# Optimizing a Trainium2 kernel written in Bass

```python
import jax, jax.numpy as jnp
from jax import lax
import numpy as np

D_MODEL = 1024
BATCH = 1
SEQ = 2048
DEPTH = 2

CTX_LEN = 256
GRID_W = 64
N_MIXERS = 2
HGRN_HEADS = 8
HGRN_HEAD_DIM = D_MODEL // HGRN_HEADS
HGRN_WIDTH = HGRN_HEADS * HGRN_HEAD_DIM
CHUNK = 64
POOL_WINDOWS = (2, 4, 8, 16)
POOL_WIDTH = D_MODEL
POOL_GROUPS = len(POOL_WINDOWS)
POOL_GROUP_DIM = POOL_WIDTH // POOL_GROUPS
N_HGRN_LAYERS = (DEPTH + 1) // 2
N_POOL_LAYERS = DEPTH // 2
EPS = 1e-6

kernel_name = 'hybrid_hgrn2_pool_prefix_dit'

def rmsnorm(x, w):
    xf = x.astype(jnp.float32)
    y = xf * lax.rsqrt(jnp.mean(xf * xf, axis=-1, keepdims=True) + EPS)
    return (y * w.astype(jnp.float32)).astype(x.dtype)

def _adaln(cond, w, b):
    mod = jax.nn.silu(cond) @ w + b
    return jnp.split(mod[:, None, :], 3, axis=-1)

def lower_bounds(logits):
    lg = jnp.concatenate([logits, jnp.zeros_like(logits[:1])], axis=0).astype(jnp.float32)
    p = jax.nn.softmax(lg, axis=0)
    return jnp.cumsum(p, axis=0)[: logits.shape[0]]

def _heads(a):
    b, t, _ = a.shape
    return a.reshape(b, t, HGRN_HEADS, HGRN_HEAD_DIM).transpose(0, 2, 1, 3)

def _chunk(a):
    b, h, t, d = a.shape
    return a.reshape(b, h, t // CHUNK, CHUNK, d)

def _inter_chunk_states(k_c, v_c, b_c, s0):
    b_last = b_c[:, :, :, -1]
    k_end = k_c * jnp.exp(b_last[:, :, :, None, :] - b_c)
    u = jnp.einsum('bhnck,bhncv->bhnkv', k_end, v_c)
    decay = jnp.exp(b_last)

    def step(s, inp):
        d_n, u_n = inp
        return d_n[..., None] * s + u_n, s

    s_final, s_prev = lax.scan(step, s0, (jnp.moveaxis(decay, 2, 0), jnp.moveaxis(u, 2, 0)))
    return jnp.moveaxis(s_prev, 0, 2), s_final

def gla_forward(q, k, v, log_f, s0):
    b, h, t, _ = q.shape
    q_c, k_c, v_c = _chunk(q), _chunk(k), _chunk(v)
    b_c = jnp.cumsum(_chunk(log_f), axis=3)
    s_prev, _ = _inter_chunk_states(k_c, v_c, b_c, s0)
    o_inter = jnp.einsum('bhnck,bhnkv->bhncv', q_c * jnp.exp(b_c), s_prev)
    b_mid = b_c[:, :, :, CHUNK // 2 - 1:CHUNK // 2]
    a = jnp.einsum('bhnck,bhnsk->bhncs', q_c * jnp.exp(b_c - b_mid), k_c * jnp.exp(b_mid - b_c))
    a = jnp.where(jnp.tril(jnp.ones((CHUNK, CHUNK), dtype=bool)), a, 0.0)
    o_intra = jnp.einsum('bhncs,bhnsv->bhncv', a, v_c)
    return (o_inter + o_intra).reshape(b, h, t, -1)

def gla_final_state(k, v, log_f, s0):
    k_c, v_c = _chunk(k), _chunk(v)
    b_c = jnp.cumsum(_chunk(log_f), axis=3)
    _, s_final = _inter_chunk_states(k_c, v_c, b_c, s0)
    return s_final

def _rev(a):
    return jnp.flip(a, axis=2)

def _hgrn2_gates(h, w_in, lb):
    f_f, f_b, i = jnp.split((h @ w_in[:, : 3 * HGRN_WIDTH]).astype(jnp.float32), 3, axis=-1)
    out = []
    for d, f_pre in enumerate((f_f, f_b)):
        f = lb[d] + (1.0 - lb[d]) * jax.nn.sigmoid(f_pre)
        out.append((_heads(1.0 - f), _heads(jnp.log(f))))
    return out[0], out[1], _heads(i)

def hgrn2_final_states(h, w_in, lb):
    (k_f, lf_f), (k_b, lf_b), v = _hgrn2_gates(h, w_in, lb)
    zeros = jnp.zeros(v.shape[:2] + (HGRN_HEAD_DIM, HGRN_HEAD_DIM), jnp.float32)
    s_f = gla_final_state(k_f, v, lf_f, zeros)
    s_b = gla_final_state(_rev(k_b), _rev(v), _rev(lf_b), zeros)
    return s_f, s_b

def hgrn2_mixer(h, w_in, lb, gnorm_w, w_out, s0_f, s0_b):
    bsz, t, _ = h.shape
    (k_f, lf_f), (k_b, lf_b), v = _hgrn2_gates(h, w_in, lb)
    q, z = jnp.split(h @ w_in[:, 3 * HGRN_WIDTH:], 2, axis=-1)
    q = _heads(jax.nn.silu(q).astype(jnp.float32)) * (HGRN_HEAD_DIM ** -0.5)
    o_f = gla_forward(q, k_f, v, lf_f, s0_f)
    o_b = _rev(gla_forward(_rev(q), _rev(k_b), _rev(v), _rev(lf_b), s0_b))
    o = (o_f + o_b).transpose(0, 2, 1, 3)
    o = rmsnorm(o, gnorm_w.reshape(HGRN_HEADS, HGRN_HEAD_DIM))
    o = o.reshape(bsz, t, HGRN_WIDTH).astype(h.dtype) * jax.nn.silu(z)
    return o @ w_out

def _centred_mean(u, w):
    length = u.shape[-2]
    csum = jnp.concatenate([jnp.zeros_like(u[..., :1, :]), jnp.cumsum(u, axis=-2)], axis=-2)
    t = jnp.arange(length)
    lo = jnp.clip(t - w // 2, 0, length)
    hi = jnp.clip(t - w // 2 + w, 0, length)
    s = jnp.take(csum, hi, axis=-2) - jnp.take(csum, lo, axis=-2)
    return s / (hi - lo).astype(u.dtype)[:, None]

def pool_mixer(h, rows, row_len, w_in, w_grp, scale, w_out):
    bsz, t, _ = h.shape
    u, z = jnp.split(h @ w_in, 2, axis=-1)
    ug = u.astype(jnp.float32).reshape(bsz, rows, row_len, POOL_GROUPS, POOL_GROUP_DIM)
    pooled = jnp.stack([_centred_mean(ug[..., g, :], w) for g, w in enumerate(POOL_WINDOWS)], axis=-2) - ug
    y = jnp.einsum('brwgi,gio->brwgo', pooled, w_grp).reshape(bsz, t, POOL_WIDTH) * scale
    return (y.astype(h.dtype) * jax.nn.silu(z)) @ w_out

def setup_inputs(seed: int = 0) -> dict:
    key = jax.random.key(seed)
    ks = jax.random.split(key, 18)
    d, e, g = D_MODEL, HGRN_WIDTH, POOL_GROUP_DIM
    n = jax.random.normal
    return {
        'x': n(ks[0], (BATCH, SEQ, d), jnp.float32),
        'c': n(ks[1], (BATCH, d), jnp.float32),
        'ctx': n(ks[2], (BATCH, CTX_LEN, d), jnp.float32),
        'c_ctx': n(ks[3], (d,), jnp.float32),
        'ada_w': n(ks[4], (DEPTH, d, 3 * d), jnp.float32) * (0.5 * d ** -0.5),
        'ada_b': n(ks[5], (DEPTH, 3 * d), jnp.float32) * 0.02,
        'norm_w': 1.0 + 0.05 * n(ks[6], (DEPTH, d), jnp.float32),
        'hgrn_w_in': n(ks[7], (N_HGRN_LAYERS, d, 5 * e), jnp.float32) * d ** -0.5,
        'hgrn_lb_logits': 0.1 * n(ks[8], (N_HGRN_LAYERS, 2, e), jnp.float32),
        'hgrn_gnorm_w': 1.0 + 0.05 * n(ks[9], (N_HGRN_LAYERS, e), jnp.float32),
        'hgrn_w_out': n(ks[10], (N_HGRN_LAYERS, e, d), jnp.float32) * e ** -0.5,
        'pool_w_in': n(ks[11], (N_POOL_LAYERS, d, 2 * POOL_WIDTH), jnp.float32) * d ** -0.5,
        'pool_w_grp': n(ks[12], (N_POOL_LAYERS, POOL_GROUPS, g, g), jnp.float32) * g ** -0.5,
        'pool_scale': 1.0 + 0.05 * n(ks[13], (N_POOL_LAYERS, POOL_WIDTH), jnp.float32),
        'pool_w_out': n(ks[14], (N_POOL_LAYERS, POOL_WIDTH, d), jnp.float32) * POOL_WIDTH ** -0.5,
        'final_norm_w': 1.0 + 0.05 * n(ks[15], (d,), jnp.float32),
    }

def reference(x, c, ctx, c_ctx, ada_w, ada_b, norm_w, hgrn_w_in, hgrn_lb_logits, hgrn_gnorm_w,
              hgrn_w_out, pool_w_in, pool_w_grp, pool_scale, pool_w_out, final_norm_w):
    rows = x.shape[1] // GRID_W
    lbs = lower_bounds(hgrn_lb_logits)
    h_ctx = ctx
    for i in range(DEPTH):
        is_hgrn = (i % N_MIXERS == 0)
        j = i // N_MIXERS
        ctx_update = any(l % N_MIXERS == 0 for l in range(i + 1, DEPTH))
        shift, scale, gate = _adaln(c, ada_w[i], ada_b[i])
        hx = rmsnorm(x, norm_w[i]) * (1.0 + scale) + shift
        if is_hgrn or ctx_update:
            c_shift, c_scale, c_gate = _adaln(c_ctx[None, :], ada_w[i], ada_b[i])
            hc = rmsnorm(h_ctx, norm_w[i]) * (1.0 + c_scale) + c_shift
        if is_hgrn:
            s_f, s_b = hgrn2_final_states(hc, hgrn_w_in[j], lbs[j])
            x = x + gate * hgrn2_mixer(hx, hgrn_w_in[j], lbs[j], hgrn_gnorm_w[j], hgrn_w_out[j], s_f, s_b)
            if ctx_update:
                zeros = jnp.zeros_like(s_f)
                h_ctx = h_ctx + c_gate * hgrn2_mixer(hc, hgrn_w_in[j], lbs[j], hgrn_gnorm_w[j], hgrn_w_out[j], zeros, zeros)
        else:
            x = x + gate * pool_mixer(hx, rows, GRID_W, pool_w_in[j], pool_w_grp[j], pool_scale[j], pool_w_out[j])
            if ctx_update:
                h_ctx = h_ctx + c_gate * pool_mixer(hc, 1, hc.shape[1], pool_w_in[j], pool_w_grp[j], pool_scale[j], pool_w_out[j])
    return rmsnorm(x, final_norm_w)


_drawn_inputs = setup_inputs


def setup_inputs(seed=0):
    import zlib

    import numpy as np

    out = dict(_drawn_inputs(seed))
    spreads = {}
    factors = {'ctx': 8.0,
     'c_ctx': 8.0,
     'norm_w': 3.191,
     'hgrn_lb_logits': 8.0,
     'hgrn_gnorm_w': 5.732,
     'pool_scale': 6.186}
    for name, (base, spread) in spreads.items():
        noise = np.random.default_rng([zlib.crc32(name.encode()), seed]).standard_normal(out[name].shape)
        drawn = base * np.exp(spread * noise) if base else spread * noise
        out[name] = __import__('jax').numpy.asarray(drawn.astype(out[name].dtype))
    for name, factor in factors.items():
        out[name] = (out[name] * factor).astype(out[name].dtype)
    return out
```

```python
import concourse.bass as bass
from concourse import mybir
from contextlib import ExitStack

FP32 = mybir.dt.float32
FP32R = mybir.dt.float32r
BF16 = mybir.dt.bfloat16
U8 = mybir.dt.uint8
ALU = mybir.AluOpType
ACT = mybir.ActivationFunctionType

P = 128
D = 1024
KT = D // P
SEQ = 2048
CTX = 256
NCOL = CTX + SEQ
BLK = 512
NBLK = SEQ // BLK
HEADS = 8
CHUNK = 64
GRID_W = 64
WINDOWS = (2, 4, 8, 16)
EPS = 1e-6
CLAMP = 2.0 ** 60

R_ADAB, R_NORM, R_GN, R_LB, R_PS, R_C, R_CC, R_ALL = 0, 48, 64, 72, 88, 96, 104, 112

GROUPS = ([("v", "c")] + [("v", b) for b in range(NBLK)] + [("q", b) for b in range(NBLK)]
          + [("f", "c")] + [("f", b) for b in range(NBLK)]
          + [("b", "c")] + [("b", b) for b in reversed(range(NBLK))]
          + [("z", b) for b in reversed(range(NBLK))])
NG = len(GROUPS)
SLICES = ["v", "q", "f", "b", "z"]
W_COL = {"f": 0, "b": 1, "v": 2, "q": 3, "z": 4}
NS = len(SLICES)
NHALF = 2 * NS
F0 = 9
X0 = 5
NV = 5
NX = NG - X0
NF = 10
NA = 8
LAST_OF = {k: max(i for i, g in enumerate(GROUPS) if g[0] == k) for k in SLICES}
assert NG == 23 and NX == 18
NLATE = 16
LCOL = 4 * D // NLATE
L0 = 2


def width(blk):
    return CTX if blk == "c" else BLK


def first_col(blk):
    return 0 if blk == "c" else CTX + blk * BLK


def chain_steps(fi):
    return sum(4 if i in (0, 5) else 8 for i in range(fi + 1))


NCHAIN = chain_steps(NF - 1)


def lat(fi):
    return None if fi in (0, 5) else (fi - 1 if fi < 5 else fi - 2)


CUTS = {0: [(0, 3), (0, 4)], 5: [(0, 5), (0, 6)], 9: [(0, 7), (0, 8)],
        14: [(0, 9), (1, 0)], 19: [(1, 1), (1, 2)]}
RING = 5


def hybrid_kernel(nc, x, ctx, ada_w, ada_late, vecs, w_in, w_out, pool_w_in, pool_w_grp, pool_w_out,
                  final_w, ident_in, mask_in, inv_in, out):
    x1_d = nc.dram_tensor("x1_scratch", (SEQ, D), FP32, kind="Internal").ap()
    gt_d = nc.dram_tensor("gated_scratch", (D, SEQ), FP32, kind="Internal").ap()
    gy_d = nc.dram_tensor("pooled_scratch", (D, SEQ), FP32, kind="Internal").ap()
    gate_d = nc.dram_tensor("gate_scratch", (32, P), FP32, kind="Internal").ap()

    es = ExitStack()
    with es:
        base0 = (nc.sbuf_base + 31) // 32 * 32
        top = nc.sbuf_usable_end
        cursor = [base0]

        def place(name, shape, dt):
            size = 4
            if dt == BF16:
                size = 2
            if dt == U8:
                size = 1
            n = size
            for s in shape[1:]:
                n *= s
            t = nc.alloc_sbuf_tensor_at(name, shape, dt, offset=cursor[0])
            cursor[0] += (n + 31) // 32 * 32
            assert cursor[0] <= top, (name, cursor[0], top)
            return t

        def sem(name):
            return es.enter_context(nc.semaphore(name))

        bank = [es.enter_context(nc.psum_tensor(f"bank{i}", [P, BLK], FP32)) for i in range(8)]
        PJ0, PJ1, TB, AB, U0, U1, OB, MB = range(8)
        MROW = (U0, OB, MB, PJ1)

        ident = place("ident", [P, P], FP32)
        mask = place("mask", [P, 2, P], U8)
        vcol = place("vcol", [P, R_ALL], FP32)
        eps = place("eps", [P, 1], FP32)
        zero_col = place("zero_col", [P, 1], FP32)
        gmul = place("gmul", [P, 3, KT], FP32)
        gadd = place("gadd", [P, 3, KT], FP32)
        head_tab = place("head_tab", [P, HEADS, 6], FP32)
        hv = place("hv", [P, 5], FP32)
        hg = place("hg", [P, 1], FP32)
        ssq = place("ssq", [P, 3, 18], FP32)
        rstd = place("rstd", [P, 3, 18], FP32)
        late = place("late", [P, 4 * KT], FP32)
        reset = place("reset", [P, BLK], BF16)
        held = cursor[0]

        h_hi = place("h_hi", [P, KT, NCOL], FP32R)
        h_lo = place("h_lo", [P, KT, NCOL], BF16)
        after_h = cursor[0]
        w_hi = place("w_hi", [P, RING, 4, P], FP32R)
        w_lo = place("w_lo", [P, RING, 4, P], FP32R)
        w_bf = place("w_bf", [P, RING, 4, P], BF16)
        w_raw = place("w_raw", [P, 2, 4, P], FP32)
        v_tok = place("v_tok", [P, 18, P], FP32)
        kp_at = cursor[0]
        kp = place("kp", [P, 2, BLK], FP32)
        start_at = cursor[0]
        q_t = place("q_t", [P, NBLK, BLK], FP32)
        o_t = place("o_t", [P, NBLK, BLK], FP32)
        xa = place("xa", [P, 2, BLK], FP32)
        xb = place("xb", [P, 2, BLK], FP32)
        qp = place("qp", [P, 2, BLK], FP32)
        q2 = place("q2", [P, 2, BLK], FP32)
        k_tok = place("k_tok", [P, 2, 4, P], FP32)
        am = place("am", [P, 4, 4, P], FP32)
        w_st = place("w_st", [P, 16, P], FP32)
        start_end = cursor[0]
        junkh = place("junkh", [P, 2, P], BF16)
        hss = place("hss", [P, 4], FP32)
        hrs = place("hrs", [P, 4], FP32)
        em = place("em", [P, 8], FP32)
        ge = place("ge", [P, NF, 9], FP32)
        cv = place("cv", [P, NF, 8], FP32)
        late_at = cursor[0]
        ada1 = place("ada1", [P, LCOL], FP32)
        cursor[0] = late_at
        grow = place("grow", [4 * KT, P], FP32)
        cursor[0] = kp_at
        v_t = place("v_t", [P, BLK], FP32)

        cursor[0] = start_at
        xt0 = place("xt0", [P, 8, D], FP32)
        junk0 = place("junk0", [P, D], BF16)
        hf0_at = cursor[0]
        hf0 = place("hf0", [P, 2, BLK], FP32)
        vrow = place("vrow", [R_ALL, P], FP32)
        sil = place("sil", [P, 3, 2 * KT], FP32)
        sil4 = place("sil4", [P, KT, 4], FP32R)
        sel = place("sel", [4, 2], FP32)
        lbt = place("lbt", [P, 5, 16], FP32)
        assert cursor[0] <= start_end
        cursor[0] = hf0_at
        maskf = place("maskf", [P, 2, P], FP32)
        cursor[0] = held
        ada_sb = place("ada_sb", [P, KT, 2, D], FP32)
        ada_hi = place("ada_hi", [P, 4, D], FP32R)
        ada_lo = place("ada_lo", [P, 4, D], FP32R)
        mrow = place("mrow", [4, 2, D], FP32)
        assert cursor[0] <= after_h

        cursor[0] = held
        h1_hi = place("h1_hi", [P, KT, SEQ], FP32R)
        h1_lo = place("h1_lo", [P, KT, SEQ], BF16)
        after_h1 = cursor[0]
        cursor[0] = after_h
        wo = place("wo", [P, KT, D], FP32)
        gateb = place("gateb", [P, D], FP32)
        og = place("og", [P, 2, KT, P], FP32)
        xr = place("xr", [P, 3, D], FP32)
        xn = place("xn", [P, 8, D], FP32)
        junk1 = place("junk1", [P, D], BF16)
        hf1_at = cursor[0]
        hf1 = place("hf1", [P, 2, BLK], FP32)
        cursor[0] = hf1_at
        fwb = place("fwb", [P, D], FP32)
        cursor[0] = after_h1
        pw_hi = place("pw_hi", [P, 8, 4, P], FP32R)
        pw_lo = place("pw_lo", [P, 8, 4, P], FP32R)
        pw_bf = place("pw_bf", [P, 8, 4, P], BF16)
        pw_raw = place("pw_raw", [P, 2, 4, P], FP32)
        py = place("py", [P, 2, 2, NBLK, BLK], FP32)
        upad = place("upad", [P, 2, 8, 80], FP32)
        dd = place("dd", [P, 2, 8, 80], FP32)
        pxa = place("pxa", [P, 2, BLK], FP32)
        pxb = place("pxb", [P, 2, BLK], FP32)
        wgrp = place("wgrp", [P, 2, 2, 2 * P], FP32)
        inv = place("inv", [P, 4, GRID_W], FP32)

        s = {}
        for n in """const_in vec_in ctx_in set_pe set_act set_dve mod_done ahi_ready alo_ready mrow_act mrow_dve tr_done hf_ready
                    h_ready w_cut w_part proj_done proj_read v_tr v_ready clamped ln1p sg_ready f_ready
                    k_ready lf_ready scanned centred e1_ready e_ready gates_x small x_done kt_tr kt_ready a_done
                    a_masked u_done w_step q2_ready o_done o_read sq_ready o_tr rs_ln rs_ready og_mul og_ready
                    late_mm late_sum late_tr late_row gate_out gate_in late_in wo_in wo_ready y_done x1_ready nrm_act xn_ready tr1_done
                    hf1_ready h1_ready pw_cut pw_part pl_chain p_ready y_mm y_read
                    pclamped pln1p psg_ready gy_ready inv_in fw_in zero_done                     fin_act head_vec c1_chain xn0 gy_mul0 h1_hi_ready cv_ready qp_ready h_mod""".split():
            s[n] = sem(n)
        for n, slots in (("ada_in", KT), ("x_in", 8), ("raw_in", 2), ("og_out", NBLK), ("ot_in", 2), ("xr_in", 3),
                         ("x1_out", 3), ("praw_in", 2), ("wgrp_in", 2), ("gy_out", 2), ("out_done", 3)):
            for i in range(slots):
                s[f"{n}{i}"] = sem(f"{n}{i}")

        block = es.enter_context(nc.Block())

        def need(e, name, per, h, c):
            v = h * per + c
            if not isinstance(v, int) or v > 0:
                e.wait_ge(s[name], v)

        def heads(e, body):
            body(0, True, False)
            with e.Fori(1, HEADS - 1) as h:
                body(h, False, False)
            body(HEADS - 1, False, True)

        NT0 = NCOL // P
        GT0 = [(0, 2)] + [(2 + 4 * b, 4) for b in range(NBLK)]

        def load_x0(sp, t):
            if t >= 8:
                g = next(i for i, (a, n) in enumerate(GT0) if a <= t - 8 < a + n)
                sp.wait_ge(s["tr_done"], KT * (g + 1))
            src = ctx[t * P:(t + 1) * P, :] if t < 2 else x[(t - 2) * P:(t - 1) * P, :]
            sp.dma_start(xt0[:, t % 8, :], src).then_inc(s[f"x_in{t % 8}"], 16)

        def store_x1(sp, t):
            sp.wait_ge(s["x1_ready"], 2 * (t + 1))
            sp.dma_start(x1_d[t * P:(t + 1) * P, :], xr[:, t % 3, :]).then_inc(s[f"x1_out{t % 3}"], 16)

        def store_gy(sp, g):
            for n in range(2 * NBLK):
                sp.wait_ge(s["gy_ready"], 2 * NBLK * g + n + 1)
                row = g * 2 * P + (n // NBLK) * P
                sp.dma_start(gy_d[row:row + P, (n % NBLK) * BLK:(n % NBLK + 1) * BLK],
                             py[:, g % 2, n // NBLK, n % NBLK, :]).then_inc(s[f"gy_out{g % 2}"], 16)

        def store_out(sp, t):
            sp.wait_ge(s["fin_act"], t + 1)
            sp.dma_start(out[t * P:(t + 1) * P, :], xr[:, t % 3, :]).then_inc(s[f"out_done{t % 3}"], 16)

        def ppool_free(act, g, n):
            act.wait_ge(s["p_ready"], 1 + g * 8 + max(n - 1, 0))

        def gy_free(act, g, n):
            if n >= 2:
                act.wait_ge(s["gy_ready"], g * 8 + n - 1)

        rms_n = [0]

        def rms(act, src, junk, row, t):
            act.activation(junk[:, :], src, ACT.Square, accum_out=ssq[:, row, t:t + 1]).then_inc(s["nrm_act"], 1)
            rms_n[0] += 1
            act.wait_ge(s["nrm_act"], rms_n[0])
            act.activation(rstd[:, row, t:t + 1], ssq[:, row, t:t + 1], ACT.Ln, scale=1.0 / D,
                           bias=eps[:, 0:1]).then_inc(s["nrm_act"], 1)
            rms_n[0] += 1
            act.wait_ge(s["nrm_act"], rms_n[0])
            act.activation(rstd[:, row, t:t + 1], rstd[:, row, t:t + 1], ACT.Exp, scale=-0.5
                           ).then_inc(s["nrm_act"], 1)
            rms_n[0] += 1

        def token_stats(act, t):
            act.wait_ge(s[f"x_in{t % 8}"], 16 * (t // 8 + 1))
            rms(act, xt0[:, t % 8, :], junk0, 0, t)

        def modulate_first(act, g):
            w = GT0[g][1] * P
            for k in range(KT):
                n = KT * g + k
                act.wait_ge(s["tr_done"], n + 1)
                if n >= 2:
                    act.wait_ge(s["hf_ready"], n - 1)
                row = 1 if g == 0 else 0
                act.activation(hf0[:, n % 2, 0:w], bank[(AB, U1)[n % 2]][:, 0:w], ACT.Identity,
                               scale=gmul[:, row, k:k + 1], bias=gadd[:, row, k:k + 1]).then_inc(s["h_mod"], 1)
                if k % 2 and g + 1 < len(GT0):
                    token_stats(act, GT0[g + 1][0] + k // 2)

        @block.sync
        def _(sp):
            sp.dma_start(vrow[:, :], vecs).then_inc(s["vec_in"], 16)
            sp.dma_start(ident[:, :], ident_in).then_inc(s["const_in"], 16)
            sp.dma_start(maskf[:, :, :], mask_in).then_inc(s["const_in"], 16)
            def load_half(h, m):
                need(sp, "w_cut", NHALF, h, m - 1)
                sp.dma_start(w_raw[:, m % 2, :, :].rearrange("p k n -> p (k n)"),
                             w_in[bass.ds(h, 1), m, :, :].rearrange("a p n -> (a p) n")).then_inc(s[f"raw_in{m % 2}"], 16)

            load_half(0, 0)
            load_half(0, 1)
            for t in range(2):
                load_x0(sp, t)
            for k in range(KT):
                sp.dma_start(ada_sb[:, k, :, :], ada_w[0, k * P:(k + 1) * P, 0:2 * D].rearrange("p (a n) -> p a n", a=2)
                             ).then_inc(s[f"ada_in{k}"], 16)
            for t in range(2, 8):
                load_x0(sp, t)
            load_half(0, 2)

            def load_late(h, i):
                need(sp, "late_mm", NLATE, h, i)
                sp.dma_start(ada1[:, :], ada_late[bass.ds(h, 1), i, :, :].rearrange("a p n -> (a p) n")
                             ).then_inc(s["late_in"], 16)

            def head(h, first, last):
                for st in range(NG):
                    for dh, m in CUTS.get(st, []):
                        if not (dh and last):
                            load_half(h + dh, m)
                    if first and st == 0:
                        for t in range(8, NT0):
                            load_x0(sp, t)
                    if L0 <= st + 1 < L0 + NLATE:
                        load_late(h, st + 1 - L0)
            heads(sp, head)

            for b in range(NBLK):
                sp.wait_ge(s[f"og_out{b}"], 16 * HEADS)
            sp.wait_ge(s["o_done"], NA * HEADS)
            sp.wait_ge(s["o_tr"], NBLK * HEADS)
            sp.dma_start(wo[:, :, :], w_out.rearrange("(k p) n -> p k n", p=P)).then_inc(s["wo_in"], 16)
            sp.wait_ge(s["gate_out"], 16)
            sp.dma_start(gateb[:, :], gate_d[0:KT, :].rearrange("(a k) n -> a (k n)", a=1).to_broadcast([P, D])).then_inc(s["gate_in"], 16)
            for t in range(SEQ // P):
                if t >= 2:
                    sp.wait_ge(s["y_done"], t - 1)
                sp.dma_start(og[:, t % 2, :, :],
                             gt_d[:, t * P:(t + 1) * P].rearrange("(k p) n -> p k n", p=P)).then_inc(s[f"ot_in{t % 2}"], 16)
                if t >= 3:
                    sp.wait_ge(s[f"x1_out{t % 3}"], 16 * (t // 3))
                    sp.wait_ge(s["xn_ready"], t - 2)
                sp.dma_start(xr[:, t % 3, :], x[t * P:(t + 1) * P, :]).then_inc(s[f"xr_in{t % 3}"], 16)
                if t >= 1:
                    store_x1(sp, t - 1)
            store_x1(sp, SEQ // P - 1)

            sp.wait_ge(s["h1_ready"], KT * NBLK)
            for i in range(3):
                sp.wait_ge(s[f"x1_out{i}"], 16 * len(range(i, SEQ // P, 3)))
            sp.dma_start(inv[:, :, :], inv_in.rearrange("(a g) w -> a g w", a=1).to_broadcast([P, 4, GRID_W])
                         ).then_inc(s["inv_in"], 16)
            pw_v = pool_w_in.rearrange("(k p) n -> p k n", p=P)
            for g in range(4):
                if g >= 2:
                    sp.wait_ge(s["y_mm"], 2 * NBLK * (g - 1))
                sp.dma_start(wgrp[:, g % 2, :, :],
                             pool_w_grp[g, :, :].rearrange("(k p) n -> p k n", p=P)).then_inc(s[f"wgrp_in{g % 2}"], 16)
                for m in range(8):
                    n = 8 * g + m
                    if n >= 2:
                        sp.wait_ge(s["pw_cut"], n - 1)
                    sl, half = m // 2, m % 2
                    col = (0 if sl < 2 else D) + g * 2 * P + (sl % 2) * P
                    sp.dma_start(pw_raw[:, n % 2, :, :],
                                 pw_v[:, 4 * half:4 * half + 4, col:col + P]).then_inc(s[f"praw_in{n % 2}"], 16)
                if g >= 1:
                    store_gy(sp, g - 1)
            store_gy(sp, 3)

            for i in range(2):
                sp.wait_ge(s[f"gy_out{i}"], 16 * 2 * NBLK * 2)
            sp.dma_start(wo[:, :, :], pool_w_out.rearrange("(k p) n -> p k n", p=P)).then_inc(s["wo_in"], 16)
            sp.dma_start(gateb[:, :], gate_d[3 * KT:4 * KT, :].rearrange("(a k) n -> a (k n)", a=1).to_broadcast([P, D])).then_inc(s["gate_in"], 16)
            sp.dma_start(fwb[:, :], final_w.to_broadcast([P, D])).then_inc(s["fw_in"], 16)
            NTL = SEQ // P
            for t in range(NTL):
                if t >= 2:
                    sp.wait_ge(s["y_done"], NTL + t - 1)
                sp.dma_start(og[:, t % 2, :, :],
                             gy_d[:, t * P:(t + 1) * P].rearrange("(k p) n -> p k n", p=P)).then_inc(s[f"ot_in{t % 2}"], 16)
                if t >= 3:
                    sp.wait_ge(s[f"out_done{t % 3}"], 16 * (t // 3))
                sp.dma_start(xr[:, t % 3, :], x1_d[t * P:(t + 1) * P, :]).then_inc(s[f"xr_in{t % 3}"], 16)
                if t >= 1:
                    store_out(sp, t - 1)
            store_out(sp, NTL - 1)
            for i in range(3):
                sp.wait_ge(s[f"out_done{i}"], 16 * len(range(i, NTL, 3)))

        @block.gpsimd
        def _(pool):
            pool.wait_ge(s["c1_chain"], 2)

            def cut_half(h, m):
                need(pool, f"raw_in{m % 2}", 8 * NHALF, h, 16 * (m // 2 + 1))
                b = m % RING
                prev = m - RING
                if prev >= 0:
                    need(pool, "proj_done", NG, h, LAST_OF[SLICES[prev // 2]] + 1)
                else:
                    need(pool, "proj_done", NG, h, LAST_OF[SLICES[(prev + NHALF) // 2]] + 1 - NG)
                raw = w_raw[:, m % 2, :, :]
                pool.tensor_tensor(w_hi[:, b, :, :], raw, zero_col[:, 0:1].unsqueeze(2).to_broadcast([P, 4, P]),
                                   ALU.add).then_inc(s["w_part"], 1)
                pool.tensor_copy(w_bf[:, b, :, :], raw).then_inc(s["w_part"], 1)
                need(pool, "w_part", 2 * NHALF, h, 2 * m + 1)
                pool.tensor_tensor(w_lo[:, b, :, :], raw, w_hi[:, b, :, :].bitcast(FP32),
                                   ALU.subtract).then_inc(s["w_cut"], 1)

            for m in range(3):
                cut_half(0, m)

            def head(h, first, last):
                for st in range(NG):
                    if first and st == NV:
                        pool.wait_ge(s["hf_ready"], KT * len(GT0))
                        for i in range(4):
                            pool.memset(am[:, i, :, :], 0.0).then_inc(s["zero_done"], 1)
                    fi = st - (F0 + 2)
                    if 0 <= fi < NF and lat(fi) is not None:
                        ai = lat(fi)
                        p = ai % 2
                        need(pool, "cv_ready", NF, h, fi + 1)
                        need(pool, "qp_ready", NA, h, ai + 1)
                        need(pool, "o_done", NA, h, ai - 1)
                        c = cv[:, fi, :] if fi < 5 else cv[:, fi, ::-1]
                        pool.tensor_tensor(q2[:, p, :].rearrange("p (c t) -> p c t", t=CHUNK),
                                           qp[:, p, :].rearrange("p (c t) -> p c t", t=CHUNK),
                                           c.unsqueeze(2).to_broadcast([P, 8, CHUNK]), ALU.mult
                                           ).then_inc(s["q2_ready"], 1)
                    for dh, m in CUTS.get(st, []):
                        if not (dh and last):
                            cut_half(h + dh, m)
            heads(pool, head)

            pool.wait_ge(s["h1_ready"], KT * NBLK)
            pool.memset(upad[:, :, :, :], 0.0).then_inc(s["p_ready"], 1)
            for n in range(32):
                pool.wait_ge(s[f"praw_in{n % 2}"], 16 * (n // 2 + 1))
                if n >= 8:
                    pool.wait_ge(s["proj_done"], HEADS * NG + NBLK * (n // 2 - 4 + 1))
                raw = pw_raw[:, n % 2, :, :]
                pool.tensor_copy(pw_hi[:, n % 8, :, :], raw).then_inc(s["pw_part"], 1)
                pool.tensor_copy(pw_bf[:, n % 8, :, :], raw).then_inc(s["pw_part"], 1)
                pool.wait_ge(s["pw_part"], 2 * n + 1)
                pool.tensor_tensor(pw_lo[:, n % 8, :, :], raw, pw_hi[:, n % 8, :, :].bitcast(FP32),
                                   ALU.subtract).then_inc(s["pw_cut"], 1)

        @block.scalar
        def _(act):
            act.preload_act_table_set("natural_log_exp_and_others")
            sa = [0]

            def step(ins):
                sa[0] += 1
                ins.then_inc(s["set_act"], 1)
                act.wait_ge(s["set_act"], sa[0])

            act.wait_ge(s["set_dve"], 1)
            step(act.activation(sil[:, 0, :], vcol[:, R_C:R_C + 16], ACT.Exp, scale=-1.0))
            for n in range(2 * KT):
                act.wait_ge(s[f"ada_in{n // 2}"], 16)
                if n >= 4:
                    act.wait_ge(s["mod_done"], n - 3)
                act.activation(ada_hi[:, n % 4, :], ada_sb[:, n // 2, n % 2, :], ACT.Copy).then_inc(s["ahi_ready"], 1)
            act.wait_ge(s["set_dve"], 2)
            step(act.activation(lbt[:, 2, :], lbt[:, 1, :], ACT.Exp))
            step(act.activation(lbt[:, 3, :], lbt[:, 0, :], ACT.Exp, scale=-1.0))
            act.wait_ge(s["mod_done"], 2 * KT)
            for i in range(2):
                act.activation(mrow[:, 0, i * BLK:(i + 1) * BLK], bank[MROW[i]][0:4, :], ACT.Copy
                               ).then_inc(s["mrow_act"], 1)
            for t in range(2):
                token_stats(act, t)
            act.wait_ge(s["set_dve"], 5)
            modulate_first(act, 0)

            def head(h, first, last):
                for st in range(NG):
                    if first and st < NBLK:
                        modulate_first(act, st + 1)
                    kind, blk = GROUPS[st]
                    w = width(blk)
                    need(act, "proj_done", NG, h, st + 1)
                    pj = bank[PJ0 + st % 2]
                    if kind == "v":
                        need(act, "v_tr", NV, h, st)
                        act.activation(v_t[:, 0:w], pj[:, 0:w], ACT.Copy).then_inc(s["proj_read"], 1)
                    else:
                        xi = st - X0
                        p = xi % 2
                        need(act, "x_done", NX, h, xi - 1)
                        ex = act.activation(xa[:, p, 0:w], pj[:, 0:w], ACT.Exp, scale=-1.0)
                        if kind in "qz":
                            act.activation(xb[:, p, 0:w], pj[:, 0:w], ACT.Copy).then_inc(s["proj_read"], 1)
                        else:
                            ex.then_inc(s["proj_read"], 1)
                    fi = st - 1 - F0
                    if 0 <= fi < NF:
                        p = (fi + 4) % 2
                        fwd = fi < 5
                        n = 4 if fi in (0, 5) else 8
                        bc = xa[:, p, 0:n * CHUNK].rearrange("p (c t) -> p c t", t=CHUNK)
                        need(act, "scanned", NF, h, fi + 1)
                        mid = bc[:, :, CHUNK // 2 - 1] if fwd else bc[:, ::-1, CHUNK // 2]
                        act.activation(em[:, 0:n], mid, ACT.Exp).then_inc(s["small"], 1)
                        need(act, "centred", NF, h, fi + 1)
                        need(act, "small", NF, h, fi + 1)
                        act.activation(xa[:, p, 0:n * CHUNK], xb[:, p, 0:n * CHUNK], ACT.Exp).then_inc(s["e1_ready"], 1)
                        act.activation(kexp(p, n), xb[:, p, 0:n * CHUNK], ACT.Exp, scale=-1.0).then_inc(s["e_ready"], 1)
                    if X0 <= st < NG:
                        xi = st - X0
                        p = xi % 2
                        kind, blk = GROUPS[st]
                        w = width(blk)
                        need(act, "clamped", NX, h, xi + 1)
                        act.activation(xa[:, p, 0:w], xa[:, p, 0:w], ACT.Ln, bias=1.0).then_inc(s["ln1p"], 1)
                        need(act, "ln1p", NX, h, xi + 1)
                        act.activation(xa[:, p, 0:w], xa[:, p, 0:w], ACT.Exp, scale=-1.0).then_inc(s["sg_ready"], 1)
                        if kind in "fb":
                            fi = st - F0
                            need(act, "f_ready", NF, h, fi + 1)
                            act.activation(xb[:, p, 0:w], xa[:, p, 0:w], ACT.Ln).then_inc(s["lf_ready"], 1)
                    fi = st - (F0 + 2)
                    if 0 <= fi < NF:
                        n = 2 if fi in (0, 5) else 4
                        need(act, "kt_tr", NF, h, fi + 1)
                        need(act, "u_done", NF, h, fi - 1)
                        act.activation(k_tok[:, fi % 2, 0:n, :],
                                       bank[TB][:, 0:n * P].rearrange("p (a b) -> p a b", b=P),
                                       ACT.Copy).then_inc(s["kt_ready"], 1)
                    if last and st == 20:
                        act.wait_ge(s["late_row"], 1)
                        act.dma_start(gate_d, grow[:, :]).then_inc(s["gate_out"], 16)
                    fi = st - (F0 + 4)
                    if 1 <= fi < 5:
                        b = GROUPS[F0 + fi][1]
                        need(act, "o_done", NA, h, fi)
                        need(act, f"og_out{b}", 16, h, 0)
                        act.activation(o_t[:, b, :], bank[OB][:, :], ACT.Copy).then_inc(s["o_read"], 1)
                    if st in (0, 2) and not first:
                        store_gated(act, h, -2 if st == 0 else -1)
                    if st >= F0 + 12:
                        store_gated(act, h, st - (F0 + 12))
                    bi = st - (F0 + 10)
                    if 0 <= bi < NBLK:
                        b = NBLK - 1 - bi
                        need(act, "o_read", NA, h, 4 + bi + 1)
                        for j in range(4):
                            if j >= 2:
                                need(act, "sq_ready", 4 * NBLK, h, 4 * bi + j - 1)
                            act.activation(junkh[:, j % 2, :], o_t[:, b, j * P:(j + 1) * P], ACT.Square,
                                           accum_out=hss[:, j:j + 1]).then_inc(s["sq_ready"], 1)
                        need(act, "sq_ready", 4 * NBLK, h, 4 * (bi + 1))
                        need(act, "og_mul", NBLK, h, bi)
                        act.activation(hrs[:, :], hss[:, :], ACT.Ln, scale=1.0 / P, bias=eps[:, 0:1]
                                       ).then_inc(s["rs_ln"], 1)
                        need(act, "rs_ln", NBLK, h, bi + 1)
                        act.activation(hrs[:, :], hrs[:, :], ACT.Exp, scale=-0.5).then_inc(s["rs_ready"], 1)

            def store_gated(act, h, bi):
                b = (NBLK - 1 - bi) % NBLK
                need(act, "og_ready", NBLK, h, bi + 1)
                row = h * P - P if bi < 0 else h * P
                act.dma_start(gt_d[bass.ds(row, P), b * BLK:(b + 1) * BLK], o_t[:, b, :]
                              ).then_inc(s[f"og_out{b}"], 16)

            def kexp(p, n):
                return xb[:, p, 0:n * CHUNK]

            heads(act, head)
            store_gated(act, HEADS, -2)
            store_gated(act, HEADS, -1)

            NTL = SEQ // P
            sa2 = [0]
            for t in range(NTL + 4):
                if t < NTL:
                    act.wait_ge(s["x1_ready"], 2 * (t + 1))
                    rms(act, xr[:, t % 3, :], junk1, 1, t)
                if t >= 4:
                    b = t // 4 - 1
                    for k in range(2 * (t % 4), 2 * (t % 4) + 2):
                        n = b * KT + k
                        act.wait_ge(s["tr1_done"], n + 1)
                        if n == 0:
                            act.wait_ge(s["set_dve"], 6)
                        if n >= 2:
                            act.wait_ge(s["h1_ready"], n - 1)
                        act.activation(hf1[:, n % 2, :], bank[TB + n % 2][:, :], ACT.Identity,
                                       scale=gmul[:, 2, k:k + 1], bias=gadd[:, 2, k:k + 1]
                                       ).then_inc(s["hf1_ready"], 1)

            with act.Fori(0, 2) as pair:
                for par in range(2):
                    g = 2 * pair + par
                    for st in range(4 * NBLK):
                        sl, b = st // NBLK, st % NBLK
                        act.wait_ge(s["proj_done"], HEADS * NG + g * 16 + st + 1)
                        pj = bank[PJ0 + st % 2]
                        if sl < 2:
                            n = st
                            ppool_free(act, g, n)
                            act.activation(upad[:, n % 2, :, 8:8 + GRID_W],
                                           pj[:, :].rearrange("p (r w) -> p r w", w=GRID_W),
                                           ACT.Copy).then_inc(s["proj_read"], 1)
                        else:
                            n = st - 8
                            gy_free(act, g, n)
                            act.activation(pxa[:, n % 2, :], pj[:, :], ACT.Exp, scale=-1.0)
                            act.activation(pxb[:, n % 2, :], pj[:, :], ACT.Copy).then_inc(s["proj_read"], 1)
                            act.wait_ge(s["pclamped"], g * 8 + n + 1)
                            act.activation(pxa[:, n % 2, :], pxa[:, n % 2, :], ACT.Ln, bias=1.0).then_inc(s["pln1p"], 1)
                            act.wait_ge(s["pln1p"], g * 8 + n + 1)
                            act.activation(pxa[:, n % 2, :], pxa[:, n % 2, :], ACT.Exp, scale=-1.0
                                           ).then_inc(s["psg_ready"], 1)

            for t in range(NTL):
                act.wait_ge(s["x1_ready"], 2 * (NTL + t + 1))
                rms(act, xr[:, t % 3, :], junk1, 2, t)

        @block.vector
        def _(dve):
            seq = [0]

            def step(ins):
                seq[0] += 1
                ins.then_inc(s["c1_chain"], 1)
                dve.wait_ge(s["c1_chain"], seq[0])

            step(dve.memset(eps[:, :], EPS))
            step(dve.memset(zero_col[:, :], 0.0))
            step(dve.memset(reset[:, :], 1.0))
            step(dve.memset(reset[:, 0:BLK:CHUNK], 0.0))
            dve.wait_ge(s["const_in"], 32)
            step(dve.tensor_copy(mask[:, :, :], maskf[:, :, :]))
            dve.wait_ge(s["set_pe"], 1)
            dve.tensor_copy(vcol[:, :], bank[TB][:, 0:R_ALL]).then_inc(s["set_dve"], 1)
            dve.wait_ge(s["set_dve"], 1)
            step(dve.tensor_scalar(lbt[:, 0, :], vcol[:, R_LB:R_LB + 16], 0.0, None, ALU.max))
            dve.tensor_tensor(lbt[:, 1, :], vcol[:, R_LB:R_LB + 16], lbt[:, 0, :], ALU.subtract
                              ).then_inc(s["set_dve"], 1)
            dve.wait_ge(s["set_act"], 1)
            step(dve.tensor_scalar(sil[:, 1, :], sil[:, 0, :], 1.0, None, ALU.add))
            step(dve.reciprocal(sil[:, 2, :], sil[:, 1, :]))
            step(dve.tensor_tensor(sil[:, 0, :], sil[:, 2, :], vcol[:, R_C:R_C + 16], ALU.mult))
            step(dve.tensor_copy(head_tab[:, :, 4], sil[:, 0, 0:KT]))
            sil2 = sil[:, 0, :].rearrange("p (a k) -> p k a", a=2)
            step(dve.tensor_tensor(sel[:, :], ident[0:4, 0:2], ident[0:4, 2:4], ALU.add))
            step(dve.tensor_copy(sil4[:, :, 0:2], sil2))
            dve.tensor_tensor(sil4[:, :, 2:4], sil2, sil4[:, :, 0:2].bitcast(FP32), ALU.subtract
                              ).then_inc(s["set_dve"], 1)
            for n in range(2 * KT):
                dve.wait_ge(s["ahi_ready"], n + 1)
                dve.tensor_tensor(ada_lo[:, n % 4, :], ada_sb[:, n // 2, n % 2, :],
                                  ada_hi[:, n % 4, :].bitcast(FP32), ALU.subtract).then_inc(s["alo_ready"], 1)
            dve.wait_ge(s["set_act"], 3)
            step(dve.tensor_tensor(lbt[:, 4, :], lbt[:, 2, :], lbt[:, 3, :], ALU.add))
            step(dve.reciprocal(lbt[:, 4, :], lbt[:, 4, :]))
            step(dve.tensor_tensor(lbt[:, 0, :], lbt[:, 2, :], lbt[:, 4, :], ALU.mult))
            for d in range(2):
                step(dve.tensor_copy(head_tab[:, :, 2 * d], lbt[:, 0, 8 * d:8 * d + 8]))
                step(dve.tensor_scalar(head_tab[:, :, 2 * d + 1], lbt[:, 0, 8 * d:8 * d + 8], -1.0, 1.0,
                                       ALU.mult, ALU.add))
            step(dve.tensor_copy(head_tab[:, :, 5], vcol[:, R_GN:R_GN + 8]))
            dve.tensor_copy(late[:, :], vcol[:, R_ADAB + 2 * KT:R_ADAB + 6 * KT]).then_inc(s["late_sum"], 1)

            dve.wait_ge(s["mod_done"], 2 * KT)
            for i in range(2):
                dve.tensor_copy(mrow[:, 1, i * BLK:(i + 1) * BLK], bank[MROW[2 + i]][0:4, :]).then_inc(s["mrow_dve"], 1)
            dve.wait_ge(s["set_pe"], 2)
            m = bank[TB][:, 0:32].rearrange("p (j a) -> p j a", a=2)
            for row in range(2):
                step(dve.tensor_tensor(gadd[:, row, :], m[:, 0:KT, row], vcol[:, R_ADAB:R_ADAB + KT], ALU.add))
                step(dve.tensor_tensor(gmul[:, row, :], m[:, KT:2 * KT, row],
                                       vcol[:, R_ADAB + KT:R_ADAB + 2 * KT], ALU.add))
                dve.scalar_tensor_tensor(gmul[:, row, :], gmul[:, row, :], 1.0, vcol[:, R_NORM:R_NORM + KT],
                                         ALU.add, ALU.mult).then_inc(s["set_dve"], 1)

            def normalise(t):
                dve.wait_ge(s["nrm_act"], 3 * (t + 1))
                dve.tensor_scalar(xt0[:, t % 8, :], xt0[:, t % 8, :], rstd[:, 0, t:t + 1], None,
                                  ALU.mult).then_inc(s["xn0"], 1)

            def split_first(g):
                t0, nt = GT0[g]
                w, col = nt * P, t0 * P
                for k in range(KT):
                    n = KT * g + k
                    dve.wait_ge(s["h_mod"], n + 1)
                    dve.tensor_copy(h_hi[:, k, col:col + w], hf0[:, n % 2, 0:w]).then_inc(s["h_ready"], 1)
                    dve.wait_ge(s["h_ready"], n + 1)
                    dve.tensor_tensor(h_lo[:, k, col:col + w], hf0[:, n % 2, 0:w],
                                      h_hi[:, k, col:col + w].bitcast(FP32), ALU.subtract
                                      ).then_inc(s["hf_ready"], 1)
                    if k % 2 and g + 1 < len(GT0):
                        normalise(GT0[g + 1][0] + k // 2)

            for t in range(2):
                normalise(t)
            split_first(0)

            def head(h, first, last):
                dve.tensor_copy(hv[:, :], head_tab[:, bass.ds(h, 1), 0:5].rearrange("p a b -> p (a b)")
                                ).then_inc(s["head_vec"], 1)
                need(dve, "head_vec", 2, h, 1)
                for st in range(NG):
                    if first and st < NBLK:
                        split_first(st + 1)
                    if first and st == F0:
                        dve.wait_ge(s["zero_done"], 4)
                    if st == L0 + NLATE:
                        need(dve, "late_mm", NLATE, h, NLATE)
                        need(dve, "late_sum", 1, h, 1)
                        dve.tensor_tensor(late[:, :], late[:, :], bank[MB][:, 0:4 * KT], ALU.add
                                          ).then_inc(s["late_sum"], 1)
                    if last and st == L0 + NLATE + 1:
                        dve.wait_ge(s["late_tr"], 1)
                        dve.tensor_copy(grow[:, :], bank[MB][0:4 * KT, 0:P]).then_inc(s["late_row"], 1)
                    if st == 0 and not first:
                        normalise_out(h, -1)
                    if st >= F0 + 11:
                        normalise_out(h, st - (F0 + 11))
                    if st == 2:
                        need(dve, "og_ready", NBLK, h, 0)
                        dve.tensor_copy(hg[:, :], head_tab[:, bass.ds(h, 1), 5]).then_inc(s["head_vec"], 1)
                    if 1 <= st <= NV:
                        j = st - 1
                        nt = 2 if j == 0 else 4
                        t0 = 0 if j == 0 else 2 + 4 * (j - 1)
                        need(dve, "v_tr", NV, h, j + 1)
                        dve.tensor_copy(v_tok[:, t0:t0 + nt, :],
                                        bank[TB][:, 0:nt * P].rearrange("p (a b) -> p a b", b=P)
                                        ).then_inc(s["v_ready"], 1)
                    if st == 1 and not first:
                        gate_out(h, -1)
                    fb = st - 1 - F0
                    if 0 <= fb < NF:
                        p = (fb + 4) % 2
                        fwd = fb < 5
                        nch = 4 if fb in (0, 5) else 8
                        a3 = xa[:, p, 0:nch * CHUNK].rearrange("p (c t) -> p c t", t=CHUNK)
                        b3 = xb[:, p, 0:nch * CHUNK].rearrange("p (c t) -> p c t", t=CHUNK)
                        mid = CHUNK // 2 - 1 if fwd else CHUNK // 2
                        need(dve, "scanned", NF, h, fb + 1)
                        dve.tensor_tensor(b3, a3, a3[:, :, mid:mid + 1].to_broadcast([P, nch, CHUNK]),
                                          ALU.subtract).then_inc(s["centred"], 1)
                    if X0 <= st < NG:
                        xi = st - X0
                        px = xi % 2
                        kind, blk = GROUPS[st]
                        w = width(blk)
                        need(dve, "proj_read", NG, h, st + 1)
                        dve.tensor_scalar(xa[:, px, 0:w], xa[:, px, 0:w], CLAMP, None, ALU.min
                                          ).then_inc(s["clamped"], 1)
                    if 0 <= fb < NF:
                        need(dve, "e_ready", NF, h, fb + 1)
                        last_t = CHUNK - 1 if fwd else 0
                        e1l = a3[:, :, last_t] if fwd else a3[:, ::-1, last_t]
                        dve.tensor_copy(ge[:, fb, 1:1 + nch], e1l).then_inc(s["gates_x"], 1)
                        if fb not in (4, 9):
                            dve.tensor_copy(ge[:, fb + 1, 0:1], e1l[:, nch - 1:nch]).then_inc(s["gates_x"], 1)
                        cnt = sum(1 if i in (4, 9) else 2 for i in range(fb + 1))
                        need(dve, "gates_x", 18, h, cnt)
                        a = 1 if fb in (0, 5) else 0
                        dve.tensor_tensor(cv[:, fb, a:nch], em[:, a:nch], ge[:, fb, a:nch], ALU.mult
                                          ).then_inc(s["cv_ready"], 1)
                        if lat(fb) is not None:
                            ai = lat(fb)
                            b = GROUPS[st - 1][1]
                            need(dve, "q2_ready", NA, h, ai - 1)
                            dve.tensor_tensor(qp[:, ai % 2, :], q_t[:, b, :], xa[:, p, :], ALU.mult
                                              ).then_inc(s["qp_ready"], 1)
                        need(dve, "k_ready", NF, h, fb + 1)
                        dve.tensor_tensor(kp[:, fb % 2, 0:nch * CHUNK], kp[:, fb % 2, 0:nch * CHUNK],
                                          xb[:, p, 0:nch * CHUNK], ALU.mult).then_inc(s["x_done"], 1)
                    if X0 <= st < NG:
                        need(dve, "sg_ready", NX, h, xi + 1)
                        if kind == "q":
                            dve.scalar_tensor_tensor(q_t[:, blk, :], xb[:, px, :], float(P) ** -0.5,
                                                     xa[:, px, :], ALU.mult, ALU.mult).then_inc(s["x_done"], 1)
                        elif kind == "z":
                            dve.tensor_tensor(q_t[:, blk, :], xb[:, px, :], xa[:, px, :], ALU.mult
                                              ).then_inc(s["x_done"], 1)
                        else:
                            fi = st - F0
                            o = 0 if kind == "f" else 2
                            dve.tensor_scalar(xa[:, px, 0:w], xa[:, px, 0:w], hv[:, o + 1:o + 2],
                                              hv[:, o:o + 1], ALU.mult, ALU.add).then_inc(s["f_ready"], 1)
                            need(dve, "f_ready", NF, h, fi + 1)
                            need(dve, "kt_tr", NF, h, fi - 1)
                            if fi >= 3:
                                need(dve, "a_done", NA, h, sum(lat(i) is not None for i in range(fi - 1)))
                            dve.tensor_scalar(kp[:, fi % 2, 0:w], xa[:, px, 0:w], -1.0, 1.0,
                                              ALU.mult, ALU.add).then_inc(s["k_ready"], 1)
                            need(dve, "k_ready", NF, h, fi + 1)
                            need(dve, "lf_ready", NF, h, fi + 1)
                            logs, sums = xb[:, px, 0:w], xa[:, px, 0:w]
                            if kind == "b":
                                logs, sums = logs[:, ::-1], sums[:, ::-1]
                            dve.tensor_tensor_scan(sums, reset[:, 0:w], logs, 0.0, ALU.mult, ALU.add
                                                   ).then_inc(s["scanned"], 1)
                    fi = st - (F0 + 4)
                    if fi >= 6:
                        ai = lat(fi)
                        b = GROUPS[F0 + fi][1]
                        need(dve, "o_done", NA, h, ai + 1)
                        dve.tensor_tensor(o_t[:, b, :], bank[OB][:, :], o_t[:, b, :], ALU.add
                                          ).then_inc(s["o_read"], 1)
                    fi = st - (F0 + 3)
                    if 0 <= fi < NF:
                        need(dve, "u_done", NF, h, fi + 1)
                        need(dve, "cv_ready", NF, h, fi + 1)
                        c0 = chain_steps(fi - 1) if fi else 0
                        nch = 4 if lat(fi) is None else 8
                        at = -4 if lat(fi) is None else 8 * lat(fi)
                        for n in range(nch):
                            c = n if fi < 5 else nch - 1 - n
                            u = bank[U0 + c % 2][:, (c // 2) * P:(c // 2 + 1) * P]
                            if n == nch - 1 and fi < NF - 1 and lat(fi + 1) is not None:
                                need(dve, "a_done", NA, h, lat(fi + 1) + 1)
                                need(dve, "o_done", NA, h, lat(fi + 1) - 1)
                            need(dve, "w_step", NCHAIN, h, c0 + n)
                            if lat(fi) is None and n == 0:
                                dve.tensor_copy(w_st[:, (at + 1) % 16, :], u).then_inc(s["w_step"], 1)
                            else:
                                dve.scalar_tensor_tensor(w_st[:, (at + n + 1) % 16, :],
                                                         w_st[:, (at + n) % 16, :], cv[:, fi, n:n + 1],
                                                         u, ALU.mult, ALU.add).then_inc(s["w_step"], 1)
                    fi = st - (F0 + 2)
                    if 0 <= fi < NF and lat(fi) is not None:
                        ai = lat(fi)
                        d = 0 if ai < 4 else 1
                        dve.copy_predicated(am[:, 2 * d + ai % 2, :, :],
                                            mask[:, d:d + 1, :].to_broadcast([P, 4, P]),
                                            bank[AB][:, :].rearrange("p (a b) -> p a b", b=P)
                                            ).then_inc(s["a_masked"], 1)
                    if st >= F0 + 11:
                        gate_out(h, st - (F0 + 11))

            def normalise_out(h, bi):
                b = (NBLK - 1 - bi) % NBLK
                need(dve, "rs_ready", NBLK, h, bi + 1)
                o = o_t[:, b, :].rearrange("p (a b) -> p a b", b=P)
                dve.tensor_tensor(o, o, hrs[:, :].unsqueeze(2).to_broadcast([P, 4, P]), ALU.mult
                                  ).then_inc(s["og_mul"], 1)

            def gate_out(h, bi):
                b = (NBLK - 1 - bi) % NBLK
                need(dve, "o_tr", NBLK, h, bi + 1)
                need(dve, "head_vec", 2, h, 0 if bi < 0 else 2)
                need(dve, "x_done", NX, h, NX - NBLK + bi + 1 if bi >= 0 else 0)
                dve.scalar_tensor_tensor(o_t[:, b, :], bank[MB][:, :], hg[:, 0:1], q_t[:, b, :],
                                         ALU.mult, ALU.mult).then_inc(s["og_ready"], 1)

            heads(dve, head)
            normalise_out(HEADS, -1)
            gate_out(HEADS, -1)

            NTL = SEQ // P

            def gate_weights(i):
                dve.wait_ge(s["wo_in"], 16 * (i + 1))
                dve.wait_ge(s["gate_in"], 16 * (i + 1))
                for k in range(KT):
                    dve.tensor_tensor(wo[:, k, :], wo[:, k, :], gateb[:, :], ALU.mult
                                      ).then_inc(s["wo_ready"], 1)

            def add_residual(i, t):
                n = NTL * i + t
                dve.wait_ge(s[f"xr_in{t % 3}"], 16 * (i * len(range(t % 3, NTL, 3)) + t // 3 + 1))
                dve.wait_ge(s["y_done"], n + 1)
                for j in range(2):
                    y = bank[(PJ0 if t % 2 == 0 else OB) + j]
                    dve.tensor_tensor(xr[:, t % 3, j * BLK:(j + 1) * BLK], y[:, :],
                                      xr[:, t % 3, j * BLK:(j + 1) * BLK], ALU.add).then_inc(s["x1_ready"], 1)

            dve.wait_ge(s["late_sum"], HEADS + 1)
            step(dve.tensor_copy(gadd[:, 2, :], late[:, KT:2 * KT]))
            dve.scalar_tensor_tensor(gmul[:, 2, :], late[:, 2 * KT:3 * KT], 1.0, vcol[:, R_NORM + KT:R_NORM + 2 * KT],
                                     ALU.add, ALU.mult).then_inc(s["set_dve"], 1)
            gate_weights(0)
            for t in range(NTL + 4):
                if t < NTL:
                    add_residual(0, t)
                    dve.wait_ge(s["nrm_act"], 3 * (NT0 + t + 1))
                    if t >= 8:
                        dve.wait_ge(s["tr1_done"], KT * (t // 4 - 1))
                    dve.tensor_scalar(xn[:, t % 8, :], xr[:, t % 3, :], rstd[:, 1, t:t + 1], None,
                                      ALU.mult).then_inc(s["xn_ready"], 1)
                if t >= 4:
                    b = t // 4 - 1
                    for k in range(2 * (t % 4), 2 * (t % 4) + 2):
                        n = b * KT + k
                        dve.wait_ge(s["hf1_ready"], n + 1)
                        dve.tensor_copy(h1_hi[:, k, b * BLK:(b + 1) * BLK], hf1[:, n % 2, :]
                                        ).then_inc(s["h1_hi_ready"], 1)
                        dve.wait_ge(s["h1_hi_ready"], n + 1)
                        dve.tensor_tensor(h1_lo[:, k, b * BLK:(b + 1) * BLK], hf1[:, n % 2, :],
                                          h1_hi[:, k, b * BLK:(b + 1) * BLK].bitcast(FP32), ALU.subtract
                                          ).then_inc(s["h1_ready"], 1)

            dve.wait_ge(s["inv_in"], 16)
            pc = [0]

            def link(ins):
                pc[0] += 1
                ins.then_inc(s["pl_chain"], 1)
                dve.wait_ge(s["pl_chain"], pc[0])

            def pool_group(g, w):
                for st in range(4 * NBLK):
                    sl, b = st // NBLK, st % NBLK
                    if sl < 2:
                        n = st
                        dve.wait_ge(s["proj_read"], HEADS * NG + 16 * g + st + 1)
                        cur = upad[:, n % 2, :, :]
                        size, i = 1, 0
                        while size < w:
                            ln = 80 - 2 * size + 1
                            link(dve.tensor_tensor(dd[:, i, :, 0:ln], cur[:, :, 0:ln], cur[:, :, size:size + ln],
                                                   ALU.add))
                            cur = dd[:, i, :, :]
                            size, i = 2 * size, 1 - i
                        tgt = dd[:, i, :, 0:GRID_W]
                        link(dve.tensor_tensor(tgt, cur[:, :, 8 - w // 2:8 - w // 2 + GRID_W],
                                               inv[:, g:g + 1, :].to_broadcast([P, 8, GRID_W]), ALU.mult))
                        if g >= 2:
                            dve.wait_ge(s[f"gy_out{g % 2}"], 16 * 8 * (g // 2))
                        dve.tensor_tensor(py[:, g % 2, sl, b, :].rearrange("p (r w) -> p r w", w=GRID_W),
                                          tgt, upad[:, n % 2, :, 8:8 + GRID_W], ALU.subtract
                                          ).then_inc(s["p_ready"], 1)
                        dve.wait_ge(s["p_ready"], 1 + 8 * g + n + 1)
                    else:
                        n = st - 8
                        o = sl - 2
                        if n < NBLK:
                            for oo in range(2):
                                dve.wait_ge(s["y_mm"], 8 * g + 2 * n + 2)
                                dve.tensor_scalar(py[:, g % 2, oo, n, :], bank[U0 + oo][:, :],
                                                  vcol[:, R_PS + 2 * g + oo:R_PS + 2 * g + oo + 1], None,
                                                  ALU.mult).then_inc(s["y_read"], 1)
                        dve.wait_ge(s["proj_read"], HEADS * NG + 16 * g + st + 1)
                        dve.tensor_scalar(pxa[:, n % 2, :], pxa[:, n % 2, :], CLAMP, None, ALU.min
                                          ).then_inc(s["pclamped"], 1)
                        dve.wait_ge(s["psg_ready"], 8 * g + n + 1)
                        dve.wait_ge(s["y_read"], 8 * g + min(2 * n + 2, 8))
                        dve.tensor_tensor(pxb[:, n % 2, :], pxb[:, n % 2, :], pxa[:, n % 2, :], ALU.mult
                                          ).then_inc(s["gy_mul0"], 1)
                        dve.wait_ge(s["gy_mul0"], 8 * g + n + 1)
                        dve.tensor_tensor(py[:, g % 2, o, b, :], py[:, g % 2, o, b, :], pxb[:, n % 2, :],
                                          ALU.mult).then_inc(s["gy_ready"], 1)
            for g, w in enumerate(WINDOWS):
                pool_group(g, w)

            gate_weights(1)
            dve.wait_ge(s["fw_in"], 16)
            for t in range(NTL):
                add_residual(1, t)
                dve.wait_ge(s["nrm_act"], 3 * (NT0 + NTL + t + 1))
                dve.wait_ge(s["x1_ready"], 2 * (NTL + t + 1))
                dve.scalar_tensor_tensor(xr[:, t % 3, :], xr[:, t % 3, :], rstd[:, 2, t:t + 1], fwb[:, :],
                                         ALU.mult, ALU.mult).then_inc(s["fin_act"], 1)

        @block.tensor
        def _(pe):
            def parts(out_ap, hi, lo, bf, m_hi, m_lo, start, stop):
                pe.matmul(out_ap, hi, m_hi, start=start, stop=False)
                pe.matmul(out_ap, bf, m_lo, start=False, stop=False)
                return pe.matmul(out_ap, lo, m_hi, start=False, stop=stop)

            pe.wait_ge(s["vec_in"], 16)
            pe.wait_ge(s["const_in"], 32)
            pe.transpose(bank[TB][:, 0:R_ALL], vrow[:, :], ident[0:R_ALL, 0:R_ALL]).then_inc(s["set_pe"], 1)
            pe.wait_ge(s["set_dve"], 3)
            for n in range(2 * KT):
                k, half = n // 2, n % 2
                pe.wait_ge(s["alo_ready"], n + 1)
                for part in (ada_hi, ada_lo):
                    for i in range(2):
                        last = pe.matmul(bank[MROW[2 * half + i]][0:4, :], sil4[:, k, :],
                                         part[:, n % 4, i * BLK:(i + 1) * BLK], start=(k == 0 and part is ada_hi),
                                         stop=(k == KT - 1 and part is ada_lo), skip_group_check=True)
                last.then_inc(s["mod_done"], 1)
            pe.wait_ge(s["mrow_act"], 2)
            pe.wait_ge(s["mrow_dve"], 2)
            for j in range(2 * KT):
                last = pe.matmul(bank[TB][:, 2 * j:2 * j + 2], mrow[:, j // KT, j % KT * P:(j % KT + 1) * P],
                                 sel[:, :], start=(j == 0), stop=True, skip_group_check=True)
            last.then_inc(s["set_pe"], 1)

            def transposes(n0, ks, tiles, src, done, ready, ready_sem, hf_sem, banks):
                pe.wait_ge(ready_sem, ready)
                for k in ks:
                    n = n0 + k
                    if n >= 2:
                        pe.wait_ge(hf_sem, n - 1)
                    for i, t in enumerate(tiles):
                        last = pe.transpose(bank[banks[n % 2]][:, i * P:(i + 1) * P],
                                            src[:, t % 8, k * P:(k + 1) * P], ident[:, :])
                    last.then_inc(done, 1)

            def transpose_first(g, ks):
                t0, nt = GT0[g]
                transposes(KT * g, ks, range(t0, t0 + nt), xt0, s["tr_done"], t0 + nt, s["xn0"], s["h_mod"],
                           (AB, U1))

            transpose_first(0, range(KT))

            def project(h, st, first):
                kind, blk = GROUPS[st]
                sl = SLICES.index(kind)
                w, col = width(blk), first_col(blk)
                if st == 0 or GROUPS[st - 1][0] != kind:
                    need(pe, "w_cut", NHALF, h, 2 * sl + 2)
                need(pe, "proj_read", NG, h, max(st - 1, 0))
                pj = bank[PJ0 + st % 2][:, 0:w]
                for k in range(KT):
                    if first and st < len(GT0):
                        if st + 1 < len(GT0):
                            transpose_first(st + 1, [k])
                        pe.wait_ge(s["hf_ready"], KT * st + k + 1)
                    b = (2 * sl + k // 4) % RING
                    last = parts(pj, w_hi[:, b, k % 4, :], w_lo[:, b, k % 4, :], w_bf[:, b, k % 4, :],
                                 h_hi[:, k, col:col + w], h_lo[:, k, col:col + w], k == 0, k == KT - 1)
                last.then_inc(s["proj_done"], 1)

            def turn_out(h, bi):
                b = (NBLK - 1 - bi) % NBLK
                need(pe, "og_mul", NBLK, h, bi + 1)
                need(pe, "og_ready", NBLK, h, bi)
                for j in range(4):
                    last = pe.transpose(bank[MB][:, j * P:(j + 1) * P], o_t[:, b, j * P:(j + 1) * P], ident[:, :])
                last.then_inc(s["o_tr"], 1)

            def head(h, first, last_head):
                for st in range(NG):
                    project(h, st, first)
                    if 1 <= st <= NV:
                        j = st - 1
                        nt = 2 if j == 0 else 4
                        need(pe, "proj_read", NG, h, st)
                        need(pe, "v_ready", NV, h, j)
                        for i in range(nt):
                            last = pe.transpose(bank[TB][:, i * P:(i + 1) * P], v_t[:, i * P:(i + 1) * P],
                                                ident[:, :])
                        last.then_inc(s["v_tr"], 1)
                    fi = st - (F0 + 4)
                    if 0 <= fi < NF and lat(fi) is not None:
                        ai = lat(fi)
                        b = GROUPS[F0 + fi][1]
                        d = 0 if ai < 4 else 1
                        need(pe, "q2_ready", NA, h, ai + 1)
                        need(pe, "w_step", NCHAIN, h, chain_steps(fi) - 1)
                        need(pe, "o_read", NA, h, ai)
                        o = bank[OB]
                        for n in range(8):
                            c = n if d == 0 else 7 - n
                            r = slice(c % 2 * CHUNK, (c % 2 + 1) * CHUNK)
                            pe.matmul(o[r, c // 2 * P:(c // 2 + 1) * P], q2[:, ai % 2, c * CHUNK:(c + 1) * CHUNK],
                                      w_st[:, (8 * ai + n) % 16, :], start=(n < 2), stop=False,
                                      skip_group_check=True)
                        need(pe, "a_masked", NA, h, ai + 1)
                        for j in range(4):
                            last = pe.matmul(o[:, j * P:(j + 1) * P], am[:, 2 * d + ai % 2, j, :],
                                             v_tok[:, 2 + 4 * b + j, :], start=False, stop=True,
                                             skip_group_check=True)
                        last.then_inc(s["o_done"], 1)
                    fi = st - (F0 + 3)
                    if 0 <= fi < NF:
                        ctxb = lat(fi) is None
                        n = 2 if ctxb else 4
                        t0 = 0 if ctxb else 2 + 4 * GROUPS[F0 + fi][1]
                        need(pe, "kt_ready", NF, h, fi + 1)
                        need(pe, "w_step", NCHAIN, h, chain_steps(fi - 1) if fi else 0)
                        for j in range(n):
                            for half in range(2):
                                r = slice(half * CHUNK, (half + 1) * CHUNK)
                                last = pe.matmul(bank[U0 + half][:, j * P:(j + 1) * P], k_tok[r, fi % 2, j, :],
                                                 v_tok[r, t0 + j, :], start=(j == 0), stop=True,
                                                 skip_group_check=True)
                        last.then_inc(s["u_done"], 1)
                    fi = st - (F0 + 2)
                    if 0 <= fi < NF:
                        n = 2 if lat(fi) is None else 4
                        need(pe, "x_done", NX, h, fi + 5)
                        if fi == 0:
                            need(pe, "v_ready", NV, h, NV)
                        for j in range(n):
                            last = pe.transpose(bank[TB][:, j * P:(j + 1) * P], kp[:, fi % 2, j * P:(j + 1) * P],
                                                ident[:, :])
                        last.then_inc(s["kt_tr"], 1)
                        if lat(fi) is not None:
                            ai = lat(fi)
                            need(pe, "a_masked", NA, h, ai)
                            for j in range(4):
                                last = pe.matmul(bank[AB][:, j * P:(j + 1) * P], kp[:, fi % 2, j * P:(j + 1) * P],
                                                 qp[:, ai % 2, j * P:(j + 1) * P], start=(j == 0), stop=True,
                                                 skip_group_check=True)
                            last.then_inc(s["a_done"], 1)
                    if st == 1 and not first:
                        turn_out(h, -1)
                    if L0 <= st < L0 + NLATE:
                        i = st - L0
                        if i == 0:
                            need(pe, "head_vec", 2, h, 1)
                            need(pe, "og_ready", NBLK, h, 0)
                        need(pe, "late_in", 16 * NLATE, h, 16 * (i + 1))
                        for j in range(LCOL // P):
                            c = i * (LCOL // P) + j
                            last = pe.matmul(bank[MB][:, c:c + 1], ada1[:, j * P:(j + 1) * P], hv[:, 4:5],
                                             start=(c == 0), stop=True, skip_group_check=True)
                        last.then_inc(s["late_mm"], 1)
                    if last_head and st == L0 + NLATE:
                        pe.wait_ge(s["late_sum"], HEADS + 1)
                        pe.transpose(bank[MB][0:4 * KT, 0:P], late[:, :], ident[:, :]).then_inc(s["late_tr"], 1)
                    if st == F0 + 11:
                        if last_head:
                            pe.wait_ge(s["late_row"], 1)
                        else:
                            need(pe, "late_sum", 1, h, 2)
                    if st >= F0 + 11:
                        turn_out(h, st - (F0 + 11))

            heads(pe, head)
            turn_out(HEADS, -1)

            NTL = SEQ // P

            def out_proj(i, t):
                n = NTL * i + t
                pe.wait_ge(s[f"ot_in{t % 2}"], 16 * (n // 2 + 1))
                if n >= 2:
                    pe.wait_ge(s["x1_ready"], 2 * (n - 1))
                for j in range(2):
                    y = bank[(PJ0 if t % 2 == 0 else OB) + j]
                    for k in range(KT):
                        if t == 0 and j == 0:
                            pe.wait_ge(s["wo_ready"], KT * i + k + 1)
                        last = pe.matmul(y[:, :], og[:, t % 2, k, :], wo[:, k, j * BLK:(j + 1) * BLK],
                                         start=(k == 0), stop=(k == KT - 1))
                last.then_inc(s["y_done"], 1)

            for t in range(NTL + 4):
                if t < NTL:
                    out_proj(0, t)
                if t >= 4:
                    b = t // 4 - 1
                    transposes(KT * b, range(2 * (t % 4), 2 * (t % 4) + 2), range(4 * b, 4 * b + 4), xn,
                               s["tr1_done"], 4 * b + 4, s["xn_ready"], s["hf1_ready"], (TB, AB))

            pe.wait_ge(s["h1_ready"], KT * NBLK)
            pe.wait_ge(s["x1_ready"], 2 * NTL)
            with pe.Fori(0, 2) as pair:
                for par in range(2):
                    g = 2 * pair + par
                    for st in range(4 * NBLK + 1):
                        if st < 4 * NBLK:
                            sl, b = st // NBLK, st % NBLK
                            if b == 0:
                                pe.wait_ge(s["pw_cut"], g * 8 + 2 * sl + 2)
                            pe.wait_ge(s["proj_read"], HEADS * NG + g * 16 + max(st - 1, 0))
                            pj = bank[PJ0 + st % 2]
                            for k in range(KT):
                                m = 2 * sl + k // 4
                                last = parts(pj[:, :], pw_hi[:, m, k % 4, :], pw_lo[:, m, k % 4, :],
                                             pw_bf[:, m, k % 4, :], h1_hi[:, k, b * BLK:(b + 1) * BLK],
                                             h1_lo[:, k, b * BLK:(b + 1) * BLK], k == 0, k == KT - 1)
                            last.then_inc(s["proj_done"], 1)
                        if 8 <= st < 12:
                            b = st - 8
                            if b == 0:
                                pe.wait_ge(s[f"wgrp_in{par}"], pair * 16 + 16)
                            pe.wait_ge(s["p_ready"], 1 + g * 8 + NBLK + b + 1)
                            if b:
                                pe.wait_ge(s["y_read"], g * 8 + 2 * b)
                            for o in range(2):
                                for k in range(2):
                                    last = pe.matmul(bank[U0 + o][:, :], wgrp[:, par, k, o * P:(o + 1) * P],
                                                     py[:, par, k, b, :],
                                                     start=(k == 0), stop=(k == 1))
                                last.then_inc(s["y_mm"], 1)

            for t in range(NTL):
                out_proj(1, t)


def kernel(**inputs):
    import numpy as _np
    import concourse.bacc as _bacc
    from concourse import mybir as _mybir
    from concourse.bass_utils import run_bass_kernel_spmd as _run

    a = {k: _np.ascontiguousarray(v) for k, v in inputs.items()}
    rows = [a["ada_b"], a["norm_w"], a["hgrn_gnorm_w"], a["hgrn_lb_logits"], a["pool_scale"], a["c"], a["c_ctx"]]
    key, query = _np.meshgrid(_np.arange(P), _np.arange(P), indexing="ij")
    same = key // CHUNK == query // CHUNK
    mask = _np.stack([same & (key <= query), same & (key >= query)], axis=1).astype(_np.float32)
    t = _np.arange(GRID_W)
    inv = _np.stack([1.0 / (_np.minimum(t - w // 2 + w, GRID_W) - _np.maximum(t - w // 2, 0))
                     for w in WINDOWS]).astype(_np.float32)
    host = [
        ("x", a["x"].reshape(SEQ, D)),
        ("ctx", a["ctx"].reshape(CTX, D)),
        ("ada_w", a["ada_w"]),
        ("ada_late", _np.concatenate([a["ada_w"][0, :, 2 * D:], a["ada_w"][1]], axis=1)
         .reshape(KT, P, NLATE, LCOL).transpose(0, 2, 1, 3)),
        ("vecs", _np.concatenate([r.reshape(-1, P) for r in rows])),
        ("w_in", a["hgrn_w_in"][0].reshape(2, 4, P, NS, HEADS, P)[:, :, :, [W_COL[k] for k in SLICES]]
         .transpose(4, 3, 0, 2, 1, 5).reshape(HEADS, NHALF, P, 4 * P)),
        ("w_out", a["hgrn_w_out"][0]),
        ("pool_w_in", a["pool_w_in"][0]),
        ("pool_w_grp", a["pool_w_grp"][0]),
        ("pool_w_out", a["pool_w_out"][0]),
        ("final_w", a["final_norm_w"].reshape(1, D)),
        ("ident", _np.eye(P, dtype=_np.float32)),
        ("mask", mask),
        ("inv", inv),
    ]
    nc = _bacc.Bacc("TRN2", target_bir_lowering=False, num_devices=1)
    arrays, args = {}, []
    for name, v in host:
        v = _np.ascontiguousarray(v)
        arrays[f"in_{name}"] = v
        args.append(nc.dram_tensor(f"in_{name}", v.shape, _mybir.dt.from_np(v.dtype), kind="ExternalInput").ap())
    args.append(nc.dram_tensor("out_0", (SEQ, D), FP32, kind="ExternalOutput").ap())
    hybrid_kernel(nc, *args)
    r = _run(nc, [arrays], core_ids=[0])
    return r.results[0]["out_0"].reshape(1, SEQ, D)
```

```python
import concourse.bass as bass
from concourse import mybir
from contextlib import ExitStack

FP32 = mybir.dt.float32
FP32R = mybir.dt.float32r
BF16 = mybir.dt.bfloat16
U8 = mybir.dt.uint8
ALU = mybir.AluOpType
ACT = mybir.ActivationFunctionType

P = 128
D = 1024
KT = D // P
SEQ = 2048
CTX = 256
NCOL = CTX + SEQ
BLK = 512
NBLK = SEQ // BLK
HEADS = 8
CHUNK = 64
GRID_W = 64
WINDOWS = (2, 4, 8, 16)
EPS = 1e-6
CLAMP = 2.0 ** 60

R_ADAB, R_NORM, R_GN, R_LB, R_PS, R_C, R_CC, R_ALL = 0, 48, 64, 72, 88, 96, 104, 112

GROUPS = ([("v", "c")] + [("v", b) for b in range(NBLK)] + [("q", b) for b in range(NBLK)]
          + [("f", "c")] + [("f", b) for b in range(NBLK)]
          + [("b", "c")] + [("b", b) for b in reversed(range(NBLK))]
          + [("z", b) for b in reversed(range(NBLK))])
NG = len(GROUPS)
SLICES = ["v", "q", "f", "b", "z"]
W_COL = {"f": 0, "b": 1, "v": 2, "q": 3, "z": 4}
NS = len(SLICES)
NHALF = 2 * NS
F0 = 9
X0 = 5
NV = 5
NX = NG - X0
NF = 10
NA = 8
LAST_OF = {k: max(i for i, g in enumerate(GROUPS) if g[0] == k) for k in SLICES}
assert NG == 23 and NX == 18
NLATE = 16
LCOL = 4 * D // NLATE
L0 = 2


def width(blk):
    return CTX if blk == "c" else BLK


def first_col(blk):
    return 0 if blk == "c" else CTX + blk * BLK


def chain_steps(fi):
    return sum(4 if i in (0, 5) else 8 for i in range(fi + 1))


NCHAIN = chain_steps(NF - 1)


def lat(fi):
    return None if fi in (0, 5) else (fi - 1 if fi < 5 else fi - 2)


CUTS = {0: [(0, 3), (0, 4)], 5: [(0, 5), (0, 6)], 9: [(0, 7), (0, 8)],
        14: [(0, 9), (1, 0)], 19: [(1, 1), (1, 2)]}
RING = 5


def hybrid_kernel(nc, x, ctx, ada_w, ada_late, vecs, w_in, w_out, pool_w_in, pool_w_grp, pool_w_out,
                  final_w, ident_in, mask_in, inv_in, out):
    x1_d = nc.dram_tensor("x1_scratch", (SEQ, D), FP32, kind="Internal").ap()
    gt_d = nc.dram_tensor("gated_scratch", (D, SEQ), FP32, kind="Internal").ap()
    gy_d = nc.dram_tensor("pooled_scratch", (D, SEQ), FP32, kind="Internal").ap()
    gate_d = nc.dram_tensor("gate_scratch", (32, P), FP32, kind="Internal").ap()

    es = ExitStack()
    with es:
        base0 = (nc.sbuf_base + 31) // 32 * 32
        top = nc.sbuf_usable_end
        cursor = [base0]

        def place(name, shape, dt):
            size = 4
            if dt == BF16:
                size = 2
            if dt == U8:
                size = 1
            n = size
            for s in shape[1:]:
                n *= s
            t = nc.alloc_sbuf_tensor_at(name, shape, dt, offset=cursor[0])
            cursor[0] += (n + 31) // 32 * 32
            assert cursor[0] <= top, (name, cursor[0], top)
            return t

        def sem(name):
            return es.enter_context(nc.semaphore(name))

        bank = [es.enter_context(nc.psum_tensor(f"bank{i}", [P, BLK], FP32)) for i in range(8)]
        PJ0, PJ1, TB, AB, U0, U1, OB, MB = range(8)
        MROW = (U0, OB, MB, PJ1)

        ident = place("ident", [P, P], FP32)
        mask = place("mask", [P, 2, P], U8)
        vcol = place("vcol", [P, R_ALL], FP32)
        eps = place("eps", [P, 1], FP32)
        zero_col = place("zero_col", [P, 1], FP32)
        gmul = place("gmul", [P, 3, KT], FP32)
        gadd = place("gadd", [P, 3, KT], FP32)
        head_tab = place("head_tab", [P, HEADS, 6], FP32)
        hv = place("hv", [P, 5], FP32)
        hg = place("hg", [P, 1], FP32)
        ssq = place("ssq", [P, 3, 18], FP32)
        rstd = place("rstd", [P, 3, 18], FP32)
        late = place("late", [P, 4 * KT], FP32)
        reset = place("reset", [P, BLK], BF16)
        held = cursor[0]

        h_hi = place("h_hi", [P, KT, NCOL], FP32R)
        h_lo = place("h_lo", [P, KT, NCOL], BF16)
        after_h = cursor[0]
        w_hi = place("w_hi", [P, RING, 4, P], FP32R)
        w_lo = place("w_lo", [P, RING, 4, P], FP32R)
        w_bf = place("w_bf", [P, RING, 4, P], BF16)
        w_raw = place("w_raw", [P, 2, 4, P], FP32)
        v_tok = place("v_tok", [P, 18, P], FP32)
        kp_at = cursor[0]
        kp = place("kp", [P, 2, BLK], FP32)
        start_at = cursor[0]
        q_t = place("q_t", [P, NBLK, BLK], FP32)
        o_t = place("o_t", [P, NBLK, BLK], FP32)
        xa = place("xa", [P, 2, BLK], FP32)
        xb = place("xb", [P, 2, BLK], FP32)
        qp = place("qp", [P, 2, BLK], FP32)
        q2 = place("q2", [P, 2, BLK], FP32)
        k_tok = place("k_tok", [P, 2, 4, P], FP32)
        am = place("am", [P, 4, 4, P], FP32)
        w_st = place("w_st", [P, 16, P], FP32)
        start_end = cursor[0]
        junkh = place("junkh", [P, 2, P], BF16)
        hss = place("hss", [P, 4], FP32)
        hrs = place("hrs", [P, 4], FP32)
        em = place("em", [P, 8], FP32)
        ge = place("ge", [P, NF, 9], FP32)
        cv = place("cv", [P, NF, 8], FP32)
        late_at = cursor[0]
        ada1 = place("ada1", [P, LCOL], FP32)
        cursor[0] = late_at
        grow = place("grow", [4 * KT, P], FP32)
        cursor[0] = kp_at
        v_t = place("v_t", [P, BLK], FP32)

        cursor[0] = start_at
        xt0 = place("xt0", [P, 8, D], FP32)
        junk0 = place("junk0", [P, D], BF16)
        hf0_at = cursor[0]
        hf0 = place("hf0", [P, 2, BLK], FP32)
        vrow = place("vrow", [R_ALL, P], FP32)
        sil = place("sil", [P, 3, 2 * KT], FP32)
        sil4 = place("sil4", [P, KT, 4], FP32R)
        sel = place("sel", [4, 2], FP32)
        lbt = place("lbt", [P, 5, 16], FP32)
        assert cursor[0] <= start_end
        cursor[0] = hf0_at
        maskf = place("maskf", [P, 2, P], FP32)
        cursor[0] = held
        ada_sb = place("ada_sb", [P, KT, 2, D], FP32)
        ada_hi = place("ada_hi", [P, 4, D], FP32R)
        ada_lo = place("ada_lo", [P, 4, D], FP32R)
        mrow = place("mrow", [4, 2, D], FP32)
        assert cursor[0] <= after_h

        cursor[0] = held
        h1_hi = place("h1_hi", [P, KT, SEQ], FP32R)
        h1_lo = place("h1_lo", [P, KT, SEQ], BF16)
        after_h1 = cursor[0]
        w_at = after_h1
        wo_hi0 = place("wo_hi0", [P, KT, D], FP32R)
        wo_lo0 = place("wo_lo0", [P, KT, D], BF16)
        gateb = place("gateb", [P, D], FP32)
        og_bf = place("og_bf", [P, 2, KT, P], BF16)
        xn = place("xn", [P, 2, D], FP32)
        hf1_at = cursor[0]
        hf1 = place("hf1", [P, 2, KT, P], FP32)
        og = place("og", [P, 2, KT, P], FP32)
        og_hi = place("og_hi", [P, 2, KT, P], FP32R)
        og_lo = place("og_lo", [P, 2, KT, P], FP32R)
        xr = place("xr", [P, 3, D], FP32)
        cursor[0] = held
        wo_raw0 = place("wo_raw0", [P, KT, NCOL], FP32)[:, :, CTX + 2 * BLK:CTX + 4 * BLK]
        cursor[0] = hf1_at
        fwb = place("fwb", [P, D], FP32)
        cursor[0] = held
        wo_raw1b = place("wo_raw1b", [P, 4, D], FP32)
        wo_hi1 = place("wo_hi1", [P, KT, D], FP32R)
        wo_lo1 = place("wo_lo1", [P, KT, D], BF16)
        assert cursor[0] <= after_h1
        cursor[0] = w_at
        wo_raw1a = place("wo_raw1a", [P, 4, D], FP32)
        wo_hi, wo_lo = (wo_hi0, wo_hi1), (wo_lo0, wo_lo1)

        def wo_raw(layer, k):
            if layer == 0:
                return wo_raw0[:, k, :]
            return wo_raw1a[:, k, :] if k < 4 else wo_raw1b[:, k - 4, :]

        def slot0(n):
            return hf1_at + (n + 1) * 2 * D * 4

        cursor[0] = w_at
        py = place("py", [P, 2, 2, NBLK, BLK], FP32)
        pw_lo_b = place("pw_lo_b", [P, 6, 4, P], FP32R)
        pw_bf_b = place("pw_bf_b", [P, 6, 4, P], BF16)
        inv = place("inv", [P, 4, GRID_W], FP32)
        cursor[0] = w_at + 13 * D * 4
        pw_bf_a = place("pw_bf_a", [P, 2, 4, P], BF16)
        pw_hi_b = place("pw_hi_b", [P, 6, 4, P], FP32R)
        wgrp = place("wgrp", [P, 2, 2, 2 * P], FP32)
        assert cursor[0] <= slot0(0)
        cursor[0] = slot0(0)
        pw_raw = place("pw_raw", [P, 2, 4, P], FP32)
        pxa = place("pxa", [P, 2, BLK], FP32)
        assert cursor[0] == slot0(1)
        pw_hi_a = place("pw_hi_a", [P, 2, 4, P], FP32R)
        pxb = place("pxb", [P, 2, BLK], FP32)
        assert cursor[0] == slot0(2)
        pw_lo_a = place("pw_lo_a", [P, 2, 4, P], FP32R)
        upad = place("upad", [P, 2, 8, 80], FP32)
        dd = place("dd", [P, 2, 8, 80], FP32)

        def pw(which, m):
            a, b = {"hi": (pw_hi_a, pw_hi_b), "lo": (pw_lo_a, pw_lo_b), "bf": (pw_bf_a, pw_bf_b)}[which]
            return a[:, m, :, :] if m < 2 else b[:, m - 2, :, :]

        s = {}
        for n in """const_in vec_in set_pe set_act set_dve mod_done ahi_ready alo_ready mrow_act mrow_dve tr_done
                    hf_ready h_ready w_cut w_part proj_done proj_read v_tr v_ready clamped ln1p sg_ready f_ready
                    k_ready lf_ready scanned centred e1_ready e_ready gates_x small x_done kt_tr kt_ready a_done
                    a_masked u_done w_step q2_ready o_done o_read sq_ready o_tr rs_ln rs_ready og_mul og_ready
                    late_mm late_sum late_tr late_row gate_out gate_in late_in ohi_ready olo_ready obf_ready
                    obf0_ready yg_ready wo_cut wo_ready y_done x1_ready nrm_act xn_ready tr1_done hf1_ready
                    h1_ready pw_cut pw_part pl_chain p_ready y_mm y_read pclamped pln1p psg_ready gy_ready inv_in
                    fw_in zero_done fin_act head_vec c1_chain xn0 gy_mul0 h1_hi_ready cv_ready qp_ready h_mod""".split():
            s[n] = sem(n)
        for n, slots in (("ada_in", KT), ("x_in", 8), ("raw_in", 2), ("og_out", NBLK), ("ot_in", 2), ("xr_in", 3),
                         ("x1_out", 3), ("praw_in", 2), ("wgrp_in", 2), ("gy_out", 2 * NBLK), ("wo_in", 4), ("out_done", 3)):
            for i in range(slots):
                s[f"{n}{i}"] = sem(f"{n}{i}")

        block = es.enter_context(nc.Block())

        def need(e, name, per, h, c):
            v = h * per + c
            if not isinstance(v, int) or v > 0:
                e.wait_ge(s[name], v)

        def heads(e, body):
            body(0, True, False)
            with e.Fori(1, HEADS - 1) as h:
                body(h, False, False)
            body(HEADS - 1, False, True)

        NT0 = NCOL // P
        NTL = SEQ // P
        GT0 = [(0, 2)] + [(2 + 4 * b, 4) for b in range(NBLK)]

        def load_x0(sp, t):
            if t >= 8:
                g = next(i for i, (a, n) in enumerate(GT0) if a <= t - 8 < a + n)
                sp.wait_ge(s["tr_done"], KT * (g + 1))
            src = ctx[t * P:(t + 1) * P, :] if t < 2 else x[(t - 2) * P:(t - 1) * P, :]
            sp.dma_start(xt0[:, t % 8, :], src).then_inc(s[f"x_in{t % 8}"], 16)

        def tile_of(i):
            return 4 * (NBLK - 1 - i // 4) + i % 4

        def bf_ready(e, layer, i):
            if i == 0:
                e.wait_ge(s["obf0_ready"], layer + 1)
            else:
                e.wait_ge(s["obf_ready"], (NTL - 1) * layer + i)

        def load_gated(sp, layer, i):
            n, t = NTL * layer + i, tile_of(i)
            if i >= 2:
                sp.wait_ge(s["olo_ready"], n - 1)
                bf_ready(sp, layer, i - 2)
            if i % 4 == 0:
                b = t // 4
                if layer == 0:
                    sp.wait_ge(s[f"og_out{b}"], 16 * HEADS)
                else:
                    for par in range(2):
                        sp.wait_ge(s[f"gy_out{NBLK * par + b}"], 16 * 2 * 2)
            src = (gt_d, gy_d)[layer]
            sp.dma_start(og[:, i % 2, :, :],
                         src[:, t * P:(t + 1) * P].rearrange("(k p) n -> p k n", p=P)).then_inc(s[f"ot_in{i % 2}"], 16)

        def store_gy(sp, g):
            for n in range(2 * NBLK):
                sp.wait_ge(s["gy_ready"], 2 * NBLK * g + n + 1)
                row = g * 2 * P + (n // NBLK) * P
                b = NBLK - 1 - n % NBLK
                sp.dma_start(gy_d[row:row + P, b * BLK:(b + 1) * BLK],
                             py[:, g % 2, n // NBLK, b, :]).then_inc(s[f"gy_out{NBLK * (g % 2) + b}"], 16)
                if g == 3 and n == NBLK + 1:
                    sp.wait_ge(s["pw_cut"], 32)
                    load_gated(sp, 1, 0)
                    t = tile_of(0)
                    sp.wait_ge(s["p_ready"], 33)
                    sp.dma_start(xr[:, 0, :], x1_d[t * P:(t + 1) * P, :]).then_inc(s["xr_in0"], 16)

        def store_out(sp, i):
            sp.wait_ge(s["fin_act"], i + 1)
            t = tile_of(i)
            sp.dma_start(out[t * P:(t + 1) * P, :], xr[:, i % 3, :]).then_inc(s[f"out_done{i % 3}"], 16)

        def ppool_free(act, g, n):
            act.wait_ge(s["p_ready"], 1 + g * 8 + max(n - 1, 0))

        def gy_free(act, g, n):
            if n >= 2:
                act.wait_ge(s["gy_ready"], g * 8 + n - 1)

        rms_n = [0]

        def rms(act, src, junk, row, t):
            act.activation(junk, src, ACT.Square, accum_out=ssq[:, row, t:t + 1]).then_inc(s["nrm_act"], 1)
            rms_n[0] += 1
            act.wait_ge(s["nrm_act"], rms_n[0])
            act.activation(rstd[:, row, t:t + 1], ssq[:, row, t:t + 1], ACT.Ln, scale=1.0 / D,
                           bias=eps[:, 0:1]).then_inc(s["nrm_act"], 1)
            rms_n[0] += 1
            act.wait_ge(s["nrm_act"], rms_n[0])
            act.activation(rstd[:, row, t:t + 1], rstd[:, row, t:t + 1], ACT.Exp, scale=-0.5
                           ).then_inc(s["nrm_act"], 1)
            rms_n[0] += 1

        def token_stats(act, t):
            act.wait_ge(s[f"x_in{t % 8}"], 16 * (t // 8 + 1))
            rms(act, xt0[:, t % 8, :], junk0[:, :], 0, t)

        def modulate_first(act, g):
            w = GT0[g][1] * P
            for k in range(KT):
                n = KT * g + k
                act.wait_ge(s["tr_done"], n + 1)
                if n >= 2:
                    act.wait_ge(s["hf_ready"], n - 1)
                row = 1 if g == 0 else 0
                act.activation(hf0[:, n % 2, 0:w], bank[(AB, U1)[n % 2]][:, 0:w], ACT.Identity,
                               scale=gmul[:, row, k:k + 1], bias=gadd[:, row, k:k + 1]).then_inc(s["h_mod"], 1)
                if k % 2 and g + 1 < len(GT0):
                    token_stats(act, GT0[g + 1][0] + k // 2)

        @block.sync
        def _(sp):
            sp.dma_start(vrow[:, :], vecs).then_inc(s["vec_in"], 16)
            sp.dma_start(ident[:, :], ident_in).then_inc(s["const_in"], 16)
            sp.dma_start(maskf[:, :, :], mask_in).then_inc(s["const_in"], 16)
            def load_half(h, m):
                need(sp, "w_cut", NHALF, h, m - 1)
                sp.dma_start(w_raw[:, m % 2, :, :].rearrange("p k n -> p (k n)"),
                             w_in[bass.ds(h, 1), m, :, :].rearrange("a p n -> (a p) n")).then_inc(s[f"raw_in{m % 2}"], 16)

            for k in range(KT):
                sp.dma_start(ada_sb[:, k, :, :], ada_w[0, k * P:(k + 1) * P, 0:2 * D].rearrange("p (a n) -> p a n", a=2)
                             ).then_inc(s[f"ada_in{k}"], 16)
            for t in range(2):
                load_x0(sp, t)
            load_half(0, 0)
            load_half(0, 1)
            for t in range(2, 8):
                load_x0(sp, t)
            load_half(0, 2)

            def load_late(h, i):
                need(sp, "late_mm", NLATE, h, i)
                sp.dma_start(ada1[:, :], ada_late[bass.ds(h, 1), i, :, :].rearrange("a p n -> (a p) n")
                             ).then_inc(s["late_in"], 16)

            def head(h, first, last):
                for st in range(NG):
                    for dh, m in CUTS.get(st, []):
                        if not (dh and last):
                            load_half(h + dh, m)
                    if first and st == 0:
                        for t in range(8, NT0):
                            load_x0(sp, t)
                    if L0 <= st + 1 < L0 + NLATE:
                        load_late(h, st + 1 - L0)
            heads(sp, head)

            sp.wait_ge(s["proj_done"], (HEADS - 1) * NG + 21)
            for j in range(4):
                sp.dma_start(wo_raw0[:, 2 * j:2 * j + 2, :],
                             w_out[2 * j * P:2 * (j + 1) * P, :].rearrange("(k p) n -> p k n", p=P)
                             ).then_inc(s[f"wo_in{j}"], 16)
            sp.wait_ge(s["x_done"], NX * HEADS)
            load_gated(sp, 0, 0)
            sp.wait_ge(s["o_done"], NA * HEADS)
            sp.wait_ge(s["og_mul"], NBLK * HEADS)
            sp.wait_ge(s["gate_out"], 16)
            sp.dma_start(gateb[:, :], gate_d[0:KT, :].rearrange("(a k) n -> a (k n)", a=1).to_broadcast([P, D])
                         ).then_inc(s["gate_in"], 16)
            for i in range(NTL):
                if i + 1 < NTL:
                    load_gated(sp, 0, i + 1)
                t = tile_of(i)
                if i >= 3:
                    sp.wait_ge(s[f"x1_out{i % 3}"], 16 * (i // 3))
                    sp.wait_ge(s["xn_ready"], i - 2)
                sp.dma_start(xr[:, i % 3, :], x[t * P:(t + 1) * P, :]).then_inc(s[f"xr_in{i % 3}"], 16)

            pw_v = pool_w_in.rearrange("(k p) n -> p k n", p=P)

            def load_slices(g, ms):
                for m in ms:
                    n = 8 * g + m
                    if n >= 2:
                        sp.wait_ge(s["pw_cut"], n - 1)
                    sl, half = m // 2, m % 2
                    col = (0 if sl < 2 else D) + g * 2 * P + (sl % 2) * P
                    sp.dma_start(pw_raw[:, n % 2, :, :],
                                 pw_v[:, 4 * half:4 * half + 4, col:col + P]).then_inc(s[f"praw_in{n % 2}"], 16)

            sp.wait_ge(s["y_done"], NTL - 1)
            load_slices(0, range(2))
            sp.wait_ge(s["h1_ready"], 2 * NTL)
            for i in range(3):
                sp.wait_ge(s[f"x1_out{i}"], 16 * len(range(i, NTL, 3)))
            sp.dma_start(inv[:, :, :], inv_in.rearrange("(a g) w -> a g w", a=1).to_broadcast([P, 4, GRID_W])
                         ).then_inc(s["inv_in"], 16)
            for g in range(4):
                if g >= 2:
                    sp.wait_ge(s["y_mm"], 2 * NBLK * (g - 1))
                sp.dma_start(wgrp[:, g % 2, :, :],
                             pool_w_grp[g, :, :].rearrange("(k p) n -> p k n", p=P)).then_inc(s[f"wgrp_in{g % 2}"], 16)
                load_slices(g, range(2 if g == 0 else 0, 8))
                if g >= 1:
                    store_gy(sp, g - 1)
            for b in range(NBLK):
                sp.wait_ge(s[f"gy_out{b}"], 16 * 2 * 2)
            w_out_v = pool_w_out.rearrange("(k p) n -> p k n", p=P)
            for j in range(2):
                sp.dma_start(wo_raw1a[:, 2 * j:2 * j + 2, :], w_out_v[:, 2 * j:2 * j + 2, :]).then_inc(s[f"wo_in{j}"], 16)
            store_gy(sp, 3)

            sp.wait_ge(s["proj_done"], HEADS * NG + 64)
            for j in range(2, 4):
                sp.dma_start(wo_raw1b[:, 2 * j - 4:2 * j - 2, :], w_out_v[:, 2 * j:2 * j + 2, :]
                             ).then_inc(s[f"wo_in{j}"], 16)
            sp.dma_start(gateb[:, :], gate_d[3 * KT:4 * KT, :].rearrange("(a k) n -> a (k n)", a=1).to_broadcast([P, D])
                         ).then_inc(s["gate_in"], 16)
            sp.dma_start(fwb[:, :], final_w.to_broadcast([P, D])).then_inc(s["fw_in"], 16)
            sp.wait_ge(s["gy_ready"], 32)
            for i in range(NTL):
                if i + 1 < NTL:
                    load_gated(sp, 1, i + 1)
                t = tile_of(i)
                if i >= 3:
                    sp.wait_ge(s[f"out_done{i % 3}"], 16 * (i // 3))
                if i >= 1:
                    sp.dma_start(xr[:, i % 3, :], x1_d[t * P:(t + 1) * P, :]).then_inc(s[f"xr_in{i % 3}"], 16)
                    store_out(sp, i - 1)
            store_out(sp, NTL - 1)
            for i in range(3):
                sp.wait_ge(s[f"out_done{i}"], 16 * len(range(i, NTL, 3)))

        @block.gpsimd
        def _(pool):
            pool.wait_ge(s["c1_chain"], 2)

            def cut_half(h, m):
                need(pool, f"raw_in{m % 2}", 8 * NHALF, h, 16 * (m // 2 + 1))
                b = m % RING
                prev = m - RING
                if prev >= 0:
                    need(pool, "proj_done", NG, h, LAST_OF[SLICES[prev // 2]] + 1)
                else:
                    need(pool, "proj_done", NG, h, LAST_OF[SLICES[(prev + NHALF) // 2]] + 1 - NG)
                raw = w_raw[:, m % 2, :, :]
                pool.tensor_tensor(w_hi[:, b, :, :], raw, zero_col[:, 0:1].unsqueeze(2).to_broadcast([P, 4, P]),
                                   ALU.add).then_inc(s["w_part"], 1)
                pool.tensor_copy(w_bf[:, b, :, :], raw).then_inc(s["w_part"], 1)
                need(pool, "w_part", 2 * NHALF, h, 2 * m + 1)
                pool.tensor_tensor(w_lo[:, b, :, :], raw, w_hi[:, b, :, :].bitcast(FP32),
                                   ALU.subtract).then_inc(s["w_cut"], 1)

            for m in range(3):
                cut_half(0, m)

            def head(h, first, last):
                for st in range(NG):
                    if first and st == NV:
                        pool.wait_ge(s["hf_ready"], KT * len(GT0))
                        for i in range(4):
                            pool.memset(am[:, i, :, :], 0.0).then_inc(s["zero_done"], 1)
                    fi = st - (F0 + 2)
                    if 0 <= fi < NF and lat(fi) is not None:
                        ai = lat(fi)
                        p = ai % 2
                        need(pool, "cv_ready", NF, h, fi + 1)
                        need(pool, "qp_ready", NA, h, ai + 1)
                        need(pool, "o_done", NA, h, ai - 1)
                        c = cv[:, fi, :] if fi < 5 else cv[:, fi, ::-1]
                        pool.tensor_tensor(q2[:, p, :].rearrange("p (c t) -> p c t", t=CHUNK),
                                           qp[:, p, :].rearrange("p (c t) -> p c t", t=CHUNK),
                                           c.unsqueeze(2).to_broadcast([P, 8, CHUNK]), ALU.mult
                                           ).then_inc(s["q2_ready"], 1)
                    for dh, m in CUTS.get(st, []):
                        if not (dh and last):
                            cut_half(h + dh, m)
            heads(pool, head)

            def round_gated(layer):
                for i in range(1, NTL):
                    n = NTL * layer + i
                    pool.wait_ge(s[f"ot_in{i % 2}"], 16 * (n // 2 + 1))
                    if i >= 2:
                        pool.wait_ge(s["y_done"], n - 1)
                    if n == 1:
                        pool.wait_ge(s["og_ready"], NBLK * HEADS)
                    pool.tensor_copy(og_bf[:, i % 2, :, :], og[:, i % 2, :, :]).then_inc(s["obf_ready"], 1)

            round_gated(0)

            for n in range(32):
                m = n % 8
                pool.wait_ge(s[f"praw_in{n % 2}"], 16 * (n // 2 + 1))
                if n == 2:
                    pool.wait_ge(s["h1_ready"], 2 * NTL)
                    pool.wait_ge(s["x1_out0"], 16 * len(range(0, NTL, 3)))
                    pool.wait_ge(s["x1_out1"], 16 * len(range(1, NTL, 3)))
                    pool.wait_ge(s["x1_out2"], 16 * len(range(2, NTL, 3)))
                    pool.memset(upad[:, :, :, :], 0.0).then_inc(s["p_ready"], 1)
                if n >= 8:
                    pool.wait_ge(s["proj_done"], HEADS * NG + NBLK * (n // 2 - 4 + 1))
                raw = pw_raw[:, n % 2, :, :]
                pool.tensor_copy(pw("hi", m), raw).then_inc(s["pw_part"], 1)
                pool.tensor_copy(pw("bf", m), raw).then_inc(s["pw_part"], 1)
                pool.wait_ge(s["pw_part"], 2 * n + 1)
                pool.tensor_tensor(pw("lo", m), raw, pw("hi", m).bitcast(FP32),
                                   ALU.subtract).then_inc(s["pw_cut"], 1)

            pool.wait_ge(s["gy_ready"], 32)
            round_gated(1)

        @block.scalar
        def _(act):
            act.preload_act_table_set("natural_log_exp_and_others")
            sa = [0]

            def step(ins):
                sa[0] += 1
                ins.then_inc(s["set_act"], 1)
                act.wait_ge(s["set_act"], sa[0])

            act.wait_ge(s["set_dve"], 1)
            step(act.activation(sil[:, 0, :], vcol[:, R_C:R_C + 16], ACT.Exp, scale=-1.0))
            for n in range(2 * KT):
                act.wait_ge(s[f"ada_in{n // 2}"], 16)
                if n >= 4:
                    act.wait_ge(s["mod_done"], n - 3)
                act.activation(ada_hi[:, n % 4, :], ada_sb[:, n // 2, n % 2, :], ACT.Copy).then_inc(s["ahi_ready"], 1)
            act.wait_ge(s["set_dve"], 2)
            step(act.activation(lbt[:, 2, :], lbt[:, 1, :], ACT.Exp))
            step(act.activation(lbt[:, 3, :], lbt[:, 0, :], ACT.Exp, scale=-1.0))
            act.wait_ge(s["mod_done"], 2 * KT)
            for i in range(2):
                act.activation(mrow[:, 0, i * BLK:(i + 1) * BLK], bank[MROW[i]][0:4, :], ACT.Copy
                               ).then_inc(s["mrow_act"], 1)
            for t in range(2):
                token_stats(act, t)
            act.wait_ge(s["set_dve"], 5)
            modulate_first(act, 0)

            def head(h, first, last):
                for st in range(NG):
                    if first and st < NBLK:
                        modulate_first(act, st + 1)
                    kind, blk = GROUPS[st]
                    w = width(blk)
                    need(act, "proj_done", NG, h, st + 1)
                    pj = bank[PJ0 + st % 2]
                    if kind == "v":
                        need(act, "v_tr", NV, h, st)
                        act.activation(v_t[:, 0:w], pj[:, 0:w], ACT.Copy).then_inc(s["proj_read"], 1)
                    else:
                        xi = st - X0
                        p = xi % 2
                        need(act, "x_done", NX, h, xi - 1)
                        ex = act.activation(xa[:, p, 0:w], pj[:, 0:w], ACT.Exp, scale=-1.0)
                        if kind in "qz":
                            act.activation(xb[:, p, 0:w], pj[:, 0:w], ACT.Copy).then_inc(s["proj_read"], 1)
                        else:
                            ex.then_inc(s["proj_read"], 1)
                    fi = st - 1 - F0
                    if 0 <= fi < NF:
                        p = (fi + 4) % 2
                        fwd = fi < 5
                        n = 4 if fi in (0, 5) else 8
                        bc = xa[:, p, 0:n * CHUNK].rearrange("p (c t) -> p c t", t=CHUNK)
                        need(act, "scanned", NF, h, fi + 1)
                        mid = bc[:, :, CHUNK // 2 - 1] if fwd else bc[:, ::-1, CHUNK // 2]
                        act.activation(em[:, 0:n], mid, ACT.Exp).then_inc(s["small"], 1)
                        need(act, "centred", NF, h, fi + 1)
                        need(act, "small", NF, h, fi + 1)
                        act.activation(xa[:, p, 0:n * CHUNK], xb[:, p, 0:n * CHUNK], ACT.Exp).then_inc(s["e1_ready"], 1)
                        act.activation(kexp(p, n), xb[:, p, 0:n * CHUNK], ACT.Exp, scale=-1.0).then_inc(s["e_ready"], 1)
                    if X0 <= st < NG:
                        xi = st - X0
                        p = xi % 2
                        kind, blk = GROUPS[st]
                        w = width(blk)
                        need(act, "clamped", NX, h, xi + 1)
                        act.activation(xa[:, p, 0:w], xa[:, p, 0:w], ACT.Ln, bias=1.0).then_inc(s["ln1p"], 1)
                        need(act, "ln1p", NX, h, xi + 1)
                        act.activation(xa[:, p, 0:w], xa[:, p, 0:w], ACT.Exp, scale=-1.0).then_inc(s["sg_ready"], 1)
                        if kind in "fb":
                            fi = st - F0
                            need(act, "f_ready", NF, h, fi + 1)
                            act.activation(xb[:, p, 0:w], xa[:, p, 0:w], ACT.Ln).then_inc(s["lf_ready"], 1)
                    fi = st - (F0 + 2)
                    if 0 <= fi < NF:
                        n = 2 if fi in (0, 5) else 4
                        need(act, "kt_tr", NF, h, fi + 1)
                        need(act, "u_done", NF, h, fi - 1)
                        act.activation(k_tok[:, fi % 2, 0:n, :],
                                       bank[TB][:, 0:n * P].rearrange("p (a b) -> p a b", b=P),
                                       ACT.Copy).then_inc(s["kt_ready"], 1)
                    if last and st == 20:
                        act.wait_ge(s["late_row"], 1)
                        act.dma_start(gate_d, grow[:, :]).then_inc(s["gate_out"], 16)
                    fi = st - (F0 + 4)
                    if 1 <= fi < 5:
                        b = GROUPS[F0 + fi][1]
                        need(act, "o_done", NA, h, fi)
                        need(act, f"og_out{b}", 16, h, 0)
                        act.activation(o_t[:, b, :], bank[OB][:, :], ACT.Copy).then_inc(s["o_read"], 1)
                    if st in (0, 2) and not first:
                        store_gated(act, h, -2 if st == 0 else -1)
                    if st >= F0 + 12:
                        store_gated(act, h, st - (F0 + 12))
                    bi = st - (F0 + 10)
                    if 0 <= bi < NBLK:
                        b = NBLK - 1 - bi
                        need(act, "o_read", NA, h, 4 + bi + 1)
                        for j in range(4):
                            if j >= 2:
                                need(act, "sq_ready", 4 * NBLK, h, 4 * bi + j - 1)
                            act.activation(junkh[:, j % 2, :], o_t[:, b, j * P:(j + 1) * P], ACT.Square,
                                           accum_out=hss[:, j:j + 1]).then_inc(s["sq_ready"], 1)
                        need(act, "sq_ready", 4 * NBLK, h, 4 * (bi + 1))
                        need(act, "og_mul", NBLK, h, bi)
                        act.activation(hrs[:, :], hss[:, :], ACT.Ln, scale=1.0 / P, bias=eps[:, 0:1]
                                       ).then_inc(s["rs_ln"], 1)
                        need(act, "rs_ln", NBLK, h, bi + 1)
                        act.activation(hrs[:, :], hrs[:, :], ACT.Exp, scale=-0.5).then_inc(s["rs_ready"], 1)

            def store_gated(act, h, bi):
                b = (NBLK - 1 - bi) % NBLK
                need(act, "og_ready", NBLK, h, bi + 1)
                row = h * P - P if bi < 0 else h * P
                act.dma_start(gt_d[bass.ds(row, P), b * BLK:(b + 1) * BLK], o_t[:, b, :]
                              ).then_inc(s[f"og_out{b}"], 16)

            def kexp(p, n):
                return xb[:, p, 0:n * CHUNK]

            heads(act, head)
            store_gated(act, HEADS, -2)

            def round_tile(layer, i):
                n = NTL * layer + i
                act.wait_ge(s[f"ot_in{i % 2}"], 16 * (n // 2 + 1))
                if i >= 2:
                    act.wait_ge(s["y_done"], n - 1)
                act.activation(og_hi[:, i % 2, :, :], og[:, i % 2, :, :], ACT.Copy).then_inc(s["ohi_ready"], 1)
                if i == 0:
                    act.activation(og_bf[:, 0, :, :], og[:, 0, :, :], ACT.Copy).then_inc(s["obf0_ready"], 1)

            def round_weights(layer, ks):
                for k in ks:
                    act.wait_ge(s[f"wo_in{k // 2}"], 16 * (layer + 1))
                    act.activation(wo_hi[layer][:, k, :], wo_raw(layer, k), ACT.Copy).then_inc(s["wo_cut"], 1)

            act.wait_ge(s["o_done"], NA * HEADS)
            round_weights(0, range(3))
            round_tile(0, 0)
            round_weights(0, range(3, KT))
            store_gated(act, HEADS, -1)
            for i in range(NTL + 1):
                if i + 1 < NTL:
                    round_tile(0, i + 1)
                if i < NTL:
                    t = tile_of(i)
                    act.wait_ge(s["x1_ready"], i + 1)
                    act.dma_start(x1_d[t * P:(t + 1) * P, :], xr[:, i % 3, :]).then_inc(s[f"x1_out{i % 3}"], 16)
                    rms(act, xr[:, i % 3, :], xn[:, i % 2, :], 1, i)
                if i == 1:
                    act.wait_ge(s["set_dve"], 6)
                if i >= 1:
                    n = i - 1
                    for k in range(KT):
                        if k % 4 == 0:
                            act.wait_ge(s["tr1_done"], 2 * n + k // 4 + 1)
                        if k == 0 and n >= 2:
                            act.wait_ge(s["h1_ready"], 2 * (n - 1))
                        mod = act.activation(hf1[:, n % 2, k, :], bank[TB + k // 4][:, k % 4 * P:(k % 4 + 1) * P],
                                             ACT.Identity, scale=gmul[:, 2, k:k + 1], bias=gadd[:, 2, k:k + 1])
                        if k % 4 == 3:
                            mod.then_inc(s["hf1_ready"], 1)

            with act.Fori(0, 2) as pair:
                for par in range(2):
                    g = 2 * pair + par
                    for st in range(4 * NBLK):
                        sl = st // NBLK
                        act.wait_ge(s["proj_done"], HEADS * NG + g * 16 + st + 1)
                        pj = bank[PJ0 + st % 2]
                        if sl < 2:
                            n = st
                            ppool_free(act, g, n)
                            act.activation(upad[:, n % 2, :, 8:8 + GRID_W],
                                           pj[:, :].rearrange("p (r w) -> p r w", w=GRID_W),
                                           ACT.Copy).then_inc(s["proj_read"], 1)
                        else:
                            n = st - 8
                            gy_free(act, g, n)
                            act.activation(pxa[:, n % 2, :], pj[:, :], ACT.Exp, scale=-1.0)
                            act.activation(pxb[:, n % 2, :], pj[:, :], ACT.Copy).then_inc(s["proj_read"], 1)
                            act.wait_ge(s["pclamped"], g * 8 + n + 1)
                            act.activation(pxa[:, n % 2, :], pxa[:, n % 2, :], ACT.Ln, bias=1.0).then_inc(s["pln1p"], 1)
                            act.wait_ge(s["pln1p"], g * 8 + n + 1)
                            act.activation(pxa[:, n % 2, :], pxa[:, n % 2, :], ACT.Exp, scale=-1.0
                                           ).then_inc(s["psg_ready"], 1)

            act.wait_ge(s["proj_done"], HEADS * NG + 52)
            round_tile(1, 0)
            act.wait_ge(s["proj_done"], HEADS * NG + 64)
            round_weights(1, range(KT))
            act.wait_ge(s["gy_ready"], 32)
            for i in range(NTL):
                if i + 1 < NTL:
                    round_tile(1, i + 1)
                act.wait_ge(s["x1_ready"], NTL + i + 1)
                rms(act, xr[:, i % 3, :], xn[:, i % 2, :], 2, i)

        @block.vector
        def _(dve):
            seq = [0]

            def step(ins):
                seq[0] += 1
                ins.then_inc(s["c1_chain"], 1)
                dve.wait_ge(s["c1_chain"], seq[0])

            step(dve.memset(eps[:, :], EPS))
            step(dve.memset(zero_col[:, :], 0.0))
            step(dve.memset(reset[:, :], 1.0))
            step(dve.memset(reset[:, 0:BLK:CHUNK], 0.0))
            dve.wait_ge(s["const_in"], 32)
            step(dve.tensor_copy(mask[:, :, :], maskf[:, :, :]))
            dve.wait_ge(s["set_pe"], 1)
            dve.tensor_copy(vcol[:, :], bank[TB][:, 0:R_ALL]).then_inc(s["set_dve"], 1)
            dve.wait_ge(s["set_dve"], 1)
            step(dve.tensor_scalar(lbt[:, 0, :], vcol[:, R_LB:R_LB + 16], 0.0, None, ALU.max))
            dve.tensor_tensor(lbt[:, 1, :], vcol[:, R_LB:R_LB + 16], lbt[:, 0, :], ALU.subtract
                              ).then_inc(s["set_dve"], 1)
            dve.wait_ge(s["set_act"], 1)
            step(dve.tensor_scalar(sil[:, 1, :], sil[:, 0, :], 1.0, None, ALU.add))
            step(dve.reciprocal(sil[:, 2, :], sil[:, 1, :]))
            step(dve.tensor_tensor(sil[:, 0, :], sil[:, 2, :], vcol[:, R_C:R_C + 16], ALU.mult))
            step(dve.tensor_copy(head_tab[:, :, 4], sil[:, 0, 0:KT]))
            sil2 = sil[:, 0, :].rearrange("p (a k) -> p k a", a=2)
            step(dve.tensor_tensor(sel[:, :], ident[0:4, 0:2], ident[0:4, 2:4], ALU.add))
            step(dve.tensor_copy(sil4[:, :, 0:2], sil2))
            dve.tensor_tensor(sil4[:, :, 2:4], sil2, sil4[:, :, 0:2].bitcast(FP32), ALU.subtract
                              ).then_inc(s["set_dve"], 1)
            for n in range(2 * KT):
                dve.wait_ge(s["ahi_ready"], n + 1)
                dve.tensor_tensor(ada_lo[:, n % 4, :], ada_sb[:, n // 2, n % 2, :],
                                  ada_hi[:, n % 4, :].bitcast(FP32), ALU.subtract).then_inc(s["alo_ready"], 1)
            dve.wait_ge(s["set_act"], 3)
            step(dve.tensor_tensor(lbt[:, 4, :], lbt[:, 2, :], lbt[:, 3, :], ALU.add))
            step(dve.reciprocal(lbt[:, 4, :], lbt[:, 4, :]))
            step(dve.tensor_tensor(lbt[:, 0, :], lbt[:, 2, :], lbt[:, 4, :], ALU.mult))
            for d in range(2):
                step(dve.tensor_copy(head_tab[:, :, 2 * d], lbt[:, 0, 8 * d:8 * d + 8]))
                step(dve.tensor_scalar(head_tab[:, :, 2 * d + 1], lbt[:, 0, 8 * d:8 * d + 8], -1.0, 1.0,
                                       ALU.mult, ALU.add))
            step(dve.tensor_copy(head_tab[:, :, 5], vcol[:, R_GN:R_GN + 8]))
            dve.tensor_copy(late[:, :], vcol[:, R_ADAB + 2 * KT:R_ADAB + 6 * KT]).then_inc(s["late_sum"], 1)

            dve.wait_ge(s["mod_done"], 2 * KT)
            for i in range(2):
                dve.tensor_copy(mrow[:, 1, i * BLK:(i + 1) * BLK], bank[MROW[2 + i]][0:4, :]).then_inc(s["mrow_dve"], 1)
            dve.wait_ge(s["set_pe"], 2)
            m = bank[TB][:, 0:32].rearrange("p (j a) -> p j a", a=2)
            for row in range(2):
                step(dve.tensor_tensor(gadd[:, row, :], m[:, 0:KT, row], vcol[:, R_ADAB:R_ADAB + KT], ALU.add))
                step(dve.tensor_tensor(gmul[:, row, :], m[:, KT:2 * KT, row],
                                       vcol[:, R_ADAB + KT:R_ADAB + 2 * KT], ALU.add))
                dve.scalar_tensor_tensor(gmul[:, row, :], gmul[:, row, :], 1.0, vcol[:, R_NORM:R_NORM + KT],
                                         ALU.add, ALU.mult).then_inc(s["set_dve"], 1)

            def normalise(t):
                dve.wait_ge(s["nrm_act"], 3 * (t + 1))
                dve.tensor_scalar(xt0[:, t % 8, :], xt0[:, t % 8, :], rstd[:, 0, t:t + 1], None,
                                  ALU.mult).then_inc(s["xn0"], 1)

            def split_first(g):
                t0, nt = GT0[g]
                w, col = nt * P, t0 * P
                for k in range(KT):
                    n = KT * g + k
                    dve.wait_ge(s["h_mod"], n + 1)
                    dve.tensor_copy(h_hi[:, k, col:col + w], hf0[:, n % 2, 0:w]).then_inc(s["h_ready"], 1)
                    dve.wait_ge(s["h_ready"], n + 1)
                    dve.tensor_tensor(h_lo[:, k, col:col + w], hf0[:, n % 2, 0:w],
                                      h_hi[:, k, col:col + w].bitcast(FP32), ALU.subtract
                                      ).then_inc(s["hf_ready"], 1)
                    if k % 2 and g + 1 < len(GT0):
                        normalise(GT0[g + 1][0] + k // 2)

            for t in range(2):
                normalise(t)
            split_first(0)

            def head(h, first, last):
                dve.tensor_copy(hv[:, :], head_tab[:, bass.ds(h, 1), 0:5].rearrange("p a b -> p (a b)")
                                ).then_inc(s["head_vec"], 1)
                need(dve, "head_vec", 2, h, 1)
                for st in range(NG):
                    if first and st < NBLK:
                        split_first(st + 1)
                    if first and st == F0:
                        dve.wait_ge(s["zero_done"], 4)
                    if st == L0 + NLATE:
                        need(dve, "late_mm", NLATE, h, NLATE)
                        need(dve, "late_sum", 1, h, 1)
                        dve.tensor_tensor(late[:, :], late[:, :], bank[MB][:, 0:4 * KT], ALU.add
                                          ).then_inc(s["late_sum"], 1)
                    if last and st == L0 + NLATE + 1:
                        dve.wait_ge(s["late_tr"], 1)
                        dve.tensor_copy(grow[:, :], bank[MB][0:4 * KT, 0:P]).then_inc(s["late_row"], 1)
                    if st == 0 and not first:
                        normalise_out(h, -1)
                    if st >= F0 + 11:
                        normalise_out(h, st - (F0 + 11))
                    if st == 2:
                        need(dve, "og_ready", NBLK, h, 0)
                        dve.tensor_copy(hg[:, :], head_tab[:, bass.ds(h, 1), 5]).then_inc(s["head_vec"], 1)
                    if 1 <= st <= NV:
                        j = st - 1
                        nt = 2 if j == 0 else 4
                        t0 = 0 if j == 0 else 2 + 4 * (j - 1)
                        need(dve, "v_tr", NV, h, j + 1)
                        dve.tensor_copy(v_tok[:, t0:t0 + nt, :],
                                        bank[TB][:, 0:nt * P].rearrange("p (a b) -> p a b", b=P)
                                        ).then_inc(s["v_ready"], 1)
                    if st == 1 and not first:
                        gate_out(h, -1)
                    fb = st - 1 - F0
                    if 0 <= fb < NF:
                        p = (fb + 4) % 2
                        fwd = fb < 5
                        nch = 4 if fb in (0, 5) else 8
                        a3 = xa[:, p, 0:nch * CHUNK].rearrange("p (c t) -> p c t", t=CHUNK)
                        b3 = xb[:, p, 0:nch * CHUNK].rearrange("p (c t) -> p c t", t=CHUNK)
                        mid = CHUNK // 2 - 1 if fwd else CHUNK // 2
                        need(dve, "scanned", NF, h, fb + 1)
                        dve.tensor_tensor(b3, a3, a3[:, :, mid:mid + 1].to_broadcast([P, nch, CHUNK]),
                                          ALU.subtract).then_inc(s["centred"], 1)
                    if X0 <= st < NG:
                        xi = st - X0
                        px = xi % 2
                        kind, blk = GROUPS[st]
                        w = width(blk)
                        need(dve, "proj_read", NG, h, st + 1)
                        dve.tensor_scalar(xa[:, px, 0:w], xa[:, px, 0:w], CLAMP, None, ALU.min
                                          ).then_inc(s["clamped"], 1)
                    if 0 <= fb < NF:
                        need(dve, "e_ready", NF, h, fb + 1)
                        last_t = CHUNK - 1 if fwd else 0
                        e1l = a3[:, :, last_t] if fwd else a3[:, ::-1, last_t]
                        dve.tensor_copy(ge[:, fb, 1:1 + nch], e1l).then_inc(s["gates_x"], 1)
                        if fb not in (4, 9):
                            dve.tensor_copy(ge[:, fb + 1, 0:1], e1l[:, nch - 1:nch]).then_inc(s["gates_x"], 1)
                        cnt = sum(1 if i in (4, 9) else 2 for i in range(fb + 1))
                        need(dve, "gates_x", 18, h, cnt)
                        a = 1 if fb in (0, 5) else 0
                        dve.tensor_tensor(cv[:, fb, a:nch], em[:, a:nch], ge[:, fb, a:nch], ALU.mult
                                          ).then_inc(s["cv_ready"], 1)
                        if lat(fb) is not None:
                            ai = lat(fb)
                            b = GROUPS[st - 1][1]
                            need(dve, "q2_ready", NA, h, ai - 1)
                            dve.tensor_tensor(qp[:, ai % 2, :], q_t[:, b, :], xa[:, p, :], ALU.mult
                                              ).then_inc(s["qp_ready"], 1)
                        need(dve, "k_ready", NF, h, fb + 1)
                        dve.tensor_tensor(kp[:, fb % 2, 0:nch * CHUNK], kp[:, fb % 2, 0:nch * CHUNK],
                                          xb[:, p, 0:nch * CHUNK], ALU.mult).then_inc(s["x_done"], 1)
                    if X0 <= st < NG:
                        need(dve, "sg_ready", NX, h, xi + 1)
                        if kind == "q":
                            dve.scalar_tensor_tensor(q_t[:, blk, :], xb[:, px, :], float(P) ** -0.5,
                                                     xa[:, px, :], ALU.mult, ALU.mult).then_inc(s["x_done"], 1)
                        elif kind == "z":
                            dve.tensor_tensor(q_t[:, blk, :], xb[:, px, :], xa[:, px, :], ALU.mult
                                              ).then_inc(s["x_done"], 1)
                        else:
                            fi = st - F0
                            o = 0 if kind == "f" else 2
                            dve.tensor_scalar(xa[:, px, 0:w], xa[:, px, 0:w], hv[:, o + 1:o + 2],
                                              hv[:, o:o + 1], ALU.mult, ALU.add).then_inc(s["f_ready"], 1)
                            need(dve, "f_ready", NF, h, fi + 1)
                            need(dve, "kt_tr", NF, h, fi - 1)
                            if fi >= 3:
                                need(dve, "a_done", NA, h, sum(lat(i) is not None for i in range(fi - 1)))
                            dve.tensor_scalar(kp[:, fi % 2, 0:w], xa[:, px, 0:w], -1.0, 1.0,
                                              ALU.mult, ALU.add).then_inc(s["k_ready"], 1)
                            need(dve, "k_ready", NF, h, fi + 1)
                            need(dve, "lf_ready", NF, h, fi + 1)
                            logs, sums = xb[:, px, 0:w], xa[:, px, 0:w]
                            if kind == "b":
                                logs, sums = logs[:, ::-1], sums[:, ::-1]
                            dve.tensor_tensor_scan(sums, reset[:, 0:w], logs, 0.0, ALU.mult, ALU.add
                                                   ).then_inc(s["scanned"], 1)
                    fi = st - (F0 + 4)
                    if fi >= 6:
                        ai = lat(fi)
                        b = GROUPS[F0 + fi][1]
                        need(dve, "o_done", NA, h, ai + 1)
                        dve.tensor_tensor(o_t[:, b, :], bank[OB][:, :], o_t[:, b, :], ALU.add
                                          ).then_inc(s["o_read"], 1)
                    fi = st - (F0 + 3)
                    if 0 <= fi < NF:
                        need(dve, "u_done", NF, h, fi + 1)
                        need(dve, "cv_ready", NF, h, fi + 1)
                        c0 = chain_steps(fi - 1) if fi else 0
                        nch = 4 if lat(fi) is None else 8
                        at = -4 if lat(fi) is None else 8 * lat(fi)
                        for n in range(nch):
                            c = n if fi < 5 else nch - 1 - n
                            u = bank[U0 + c % 2][:, (c // 2) * P:(c // 2 + 1) * P]
                            if n == nch - 1 and fi < NF - 1 and lat(fi + 1) is not None:
                                need(dve, "a_done", NA, h, lat(fi + 1) + 1)
                                need(dve, "o_done", NA, h, lat(fi + 1) - 1)
                            need(dve, "w_step", NCHAIN, h, c0 + n)
                            if lat(fi) is None and n == 0:
                                dve.tensor_copy(w_st[:, (at + 1) % 16, :], u).then_inc(s["w_step"], 1)
                            else:
                                dve.scalar_tensor_tensor(w_st[:, (at + n + 1) % 16, :],
                                                         w_st[:, (at + n) % 16, :], cv[:, fi, n:n + 1],
                                                         u, ALU.mult, ALU.add).then_inc(s["w_step"], 1)
                    fi = st - (F0 + 2)
                    if 0 <= fi < NF and lat(fi) is not None:
                        ai = lat(fi)
                        d = 0 if ai < 4 else 1
                        dve.copy_predicated(am[:, 2 * d + ai % 2, :, :],
                                            mask[:, d:d + 1, :].to_broadcast([P, 4, P]),
                                            bank[AB][:, :].rearrange("p (a b) -> p a b", b=P)
                                            ).then_inc(s["a_masked"], 1)
                    if st >= F0 + 11:
                        gate_out(h, st - (F0 + 11))

            def normalise_out(h, bi):
                b = (NBLK - 1 - bi) % NBLK
                need(dve, "rs_ready", NBLK, h, bi + 1)
                o = o_t[:, b, :].rearrange("p (a b) -> p a b", b=P)
                dve.tensor_tensor(o, o, hrs[:, :].unsqueeze(2).to_broadcast([P, 4, P]), ALU.mult
                                  ).then_inc(s["og_mul"], 1)

            def gate_out(h, bi):
                b = (NBLK - 1 - bi) % NBLK
                need(dve, "o_tr", NBLK, h, bi + 1)
                need(dve, "head_vec", 2, h, 0 if bi < 0 else 2)
                need(dve, "x_done", NX, h, NX - NBLK + bi + 1 if bi >= 0 else 0)
                dve.scalar_tensor_tensor(o_t[:, b, :], bank[MB][:, :], hg[:, 0:1], q_t[:, b, :],
                                         ALU.mult, ALU.mult).then_inc(s["og_ready"], 1)

            heads(dve, head)
            normalise_out(HEADS, -1)

            dve.wait_ge(s["late_sum"], HEADS + 1)
            step(dve.tensor_copy(gadd[:, 2, :], late[:, KT:2 * KT]))
            dve.scalar_tensor_tensor(gmul[:, 2, :], late[:, 2 * KT:3 * KT], 1.0, vcol[:, R_NORM + KT:R_NORM + 2 * KT],
                                     ALU.add, ALU.mult).then_inc(s["set_dve"], 1)

            def rest_weights(layer, ks):
                for k in ks:
                    dve.wait_ge(s["wo_cut"], KT * layer + k + 1)
                    dve.tensor_tensor(wo_lo[layer][:, k, :], wo_raw(layer, k),
                                      wo_hi[layer][:, k, :].bitcast(FP32), ALU.subtract).then_inc(s["wo_ready"], 1)

            def rest_tile(layer, i):
                n = NTL * layer + i
                dve.wait_ge(s["ohi_ready"], n + 1)
                dve.tensor_tensor(og_lo[:, i % 2, :, :], og[:, i % 2, :, :], og_hi[:, i % 2, :, :].bitcast(FP32),
                                  ALU.subtract).then_inc(s["olo_ready"], 1)

            def add_residual(layer, i):
                n = NTL * layer + i
                dve.wait_ge(s["y_done"], n + 1)
                for j in range(2):
                    y = bank[(PJ0 if i % 2 == 0 else OB) + j]
                    c = slice(j * BLK, (j + 1) * BLK)
                    dve.tensor_tensor(xn[:, i % 2, c], y[:, :], gateb[:, c], ALU.mult).then_inc(s["yg_ready"], 1)
                dve.wait_ge(s[f"xr_in{i % 3}"], 16 * (layer * len(range(i % 3, NTL, 3)) + i // 3 + 1))
                dve.wait_ge(s["yg_ready"], 2 * n + 2)
                dve.tensor_tensor(xr[:, i % 3, :], xr[:, i % 3, :], xn[:, i % 2, :], ALU.add).then_inc(s["x1_ready"], 1)

            rest_weights(0, range(3))
            rest_tile(0, 0)
            rest_weights(0, range(3, KT))
            gate_out(HEADS, -1)
            for b in range(NBLK):
                dve.wait_ge(s[f"og_out{b}"], 16 * HEADS)
            dve.wait_ge(s["gate_in"], 16)
            for i in range(NTL + 1):
                if i + 1 < NTL:
                    rest_tile(0, i + 1)
                if i < NTL:
                    if i >= 2:
                        dve.wait_ge(s["tr1_done"], 2 * (i - 1))
                    add_residual(0, i)
                    dve.wait_ge(s["nrm_act"], 3 * (NT0 + i + 1))
                    dve.tensor_scalar(xn[:, i % 2, :], xr[:, i % 3, :], rstd[:, 1, i:i + 1], None,
                                      ALU.mult).then_inc(s["xn_ready"], 1)
                if i >= 1:
                    n = i - 1
                    cols = slice(tile_of(n) * P, (tile_of(n) + 1) * P)
                    for j in range(2):
                        ks = slice(4 * j, 4 * j + 4)
                        dve.wait_ge(s["hf1_ready"], 2 * n + j + 1)
                        dve.tensor_copy(h1_hi[:, ks, cols], hf1[:, n % 2, ks, :]).then_inc(s["h1_hi_ready"], 1)
                        dve.wait_ge(s["h1_hi_ready"], 2 * n + j + 1)
                        dve.tensor_tensor(h1_lo[:, ks, cols], hf1[:, n % 2, ks, :],
                                          h1_hi[:, ks, cols].bitcast(FP32), ALU.subtract).then_inc(s["h1_ready"], 1)

            dve.wait_ge(s["inv_in"], 16)
            pc = [0]

            def link(ins):
                pc[0] += 1
                ins.then_inc(s["pl_chain"], 1)
                dve.wait_ge(s["pl_chain"], pc[0])

            def pool_group(g, w):
                for st in range(4 * NBLK):
                    sl, b = st // NBLK, NBLK - 1 - st % NBLK
                    if sl < 2:
                        n = st
                        dve.wait_ge(s["proj_read"], HEADS * NG + 16 * g + st + 1)
                        cur = upad[:, n % 2, :, :]
                        size, i = 1, 0
                        while size < w:
                            ln = 80 - 2 * size + 1
                            link(dve.tensor_tensor(dd[:, i, :, 0:ln], cur[:, :, 0:ln], cur[:, :, size:size + ln],
                                                   ALU.add))
                            cur = dd[:, i, :, :]
                            size, i = 2 * size, 1 - i
                        tgt = dd[:, i, :, 0:GRID_W]
                        link(dve.tensor_tensor(tgt, cur[:, :, 8 - w // 2:8 - w // 2 + GRID_W],
                                               inv[:, g:g + 1, :].to_broadcast([P, 8, GRID_W]), ALU.mult))
                        if g >= 2:
                            dve.wait_ge(s[f"gy_out{NBLK * (g % 2) + b}"], 16 * 2 * (g // 2))
                        dve.tensor_tensor(py[:, g % 2, sl, b, :].rearrange("p (r w) -> p r w", w=GRID_W),
                                          tgt, upad[:, n % 2, :, 8:8 + GRID_W], ALU.subtract
                                          ).then_inc(s["p_ready"], 1)
                        dve.wait_ge(s["p_ready"], 1 + 8 * g + n + 1)
                    else:
                        n = st - 8
                        o = sl - 2
                        if n < NBLK:
                            for oo in range(2):
                                dve.wait_ge(s["y_mm"], 8 * g + 2 * n + 2)
                                dve.tensor_scalar(py[:, g % 2, oo, b, :], bank[U0 + oo][:, :],
                                                  vcol[:, R_PS + 2 * g + oo:R_PS + 2 * g + oo + 1], None,
                                                  ALU.mult).then_inc(s["y_read"], 1)
                        dve.wait_ge(s["proj_read"], HEADS * NG + 16 * g + st + 1)
                        dve.tensor_scalar(pxa[:, n % 2, :], pxa[:, n % 2, :], CLAMP, None, ALU.min
                                          ).then_inc(s["pclamped"], 1)
                        dve.wait_ge(s["psg_ready"], 8 * g + n + 1)
                        dve.wait_ge(s["y_read"], 8 * g + min(2 * n + 2, 8))
                        dve.tensor_tensor(pxb[:, n % 2, :], pxb[:, n % 2, :], pxa[:, n % 2, :], ALU.mult
                                          ).then_inc(s["gy_mul0"], 1)
                        dve.wait_ge(s["gy_mul0"], 8 * g + n + 1)
                        dve.tensor_tensor(py[:, g % 2, o, b, :], py[:, g % 2, o, b, :], pxb[:, n % 2, :],
                                          ALU.mult).then_inc(s["gy_ready"], 1)
            for g, w in enumerate(WINDOWS):
                pool_group(g, w)

            rest_tile(1, 0)
            rest_weights(1, range(KT))
            dve.wait_ge(s["gate_in"], 32)
            dve.wait_ge(s["fw_in"], 16)
            for i in range(NTL):
                if i + 1 < NTL:
                    rest_tile(1, i + 1)
                add_residual(1, i)
                dve.wait_ge(s["nrm_act"], 3 * (NT0 + NTL + i + 1))
                dve.wait_ge(s["x1_ready"], NTL + i + 1)
                dve.scalar_tensor_tensor(xr[:, i % 3, :], xr[:, i % 3, :], rstd[:, 2, i:i + 1], fwb[:, :],
                                         ALU.mult, ALU.mult).then_inc(s["fin_act"], 1)

        @block.tensor
        def _(pe):
            def parts(out_ap, hi, lo, bf, m_hi, m_lo, start, stop):
                pe.matmul(out_ap, hi, m_hi, start=start, stop=False)
                pe.matmul(out_ap, bf, m_lo, start=False, stop=False)
                return pe.matmul(out_ap, lo, m_hi, start=False, stop=stop)

            pe.wait_ge(s["vec_in"], 16)
            pe.wait_ge(s["const_in"], 32)
            pe.transpose(bank[TB][:, 0:R_ALL], vrow[:, :], ident[0:R_ALL, 0:R_ALL]).then_inc(s["set_pe"], 1)
            pe.wait_ge(s["set_dve"], 3)
            for n in range(2 * KT):
                k, half = n // 2, n % 2
                pe.wait_ge(s["alo_ready"], n + 1)
                for part in (ada_hi, ada_lo):
                    for i in range(2):
                        last = pe.matmul(bank[MROW[2 * half + i]][0:4, :], sil4[:, k, :],
                                         part[:, n % 4, i * BLK:(i + 1) * BLK], start=(k == 0 and part is ada_hi),
                                         stop=(k == KT - 1 and part is ada_lo), skip_group_check=True)
                last.then_inc(s["mod_done"], 1)
            pe.wait_ge(s["mrow_act"], 2)
            pe.wait_ge(s["mrow_dve"], 2)
            for j in range(2 * KT):
                last = pe.matmul(bank[TB][:, 2 * j:2 * j + 2], mrow[:, j // KT, j % KT * P:(j % KT + 1) * P],
                                 sel[:, :], start=(j == 0), stop=True, skip_group_check=True)
            last.then_inc(s["set_pe"], 1)

            def transposes(n0, ks, tiles, src, done, ready, ready_sem, hf_sem, banks):
                pe.wait_ge(ready_sem, ready)
                for k in ks:
                    n = n0 + k
                    if n >= 2:
                        pe.wait_ge(hf_sem, n - 1)
                    for i, t in enumerate(tiles):
                        last = pe.transpose(bank[banks[n % 2]][:, i * P:(i + 1) * P],
                                            src[:, t % 8, k * P:(k + 1) * P], ident[:, :])
                    last.then_inc(done, 1)

            def transpose_first(g, ks):
                t0, nt = GT0[g]
                transposes(KT * g, ks, range(t0, t0 + nt), xt0, s["tr_done"], t0 + nt, s["xn0"], s["h_mod"],
                           (AB, U1))

            transpose_first(0, range(KT))

            def project(h, st, first):
                kind, blk = GROUPS[st]
                sl = SLICES.index(kind)
                w, col = width(blk), first_col(blk)
                if st == 0 or GROUPS[st - 1][0] != kind:
                    need(pe, "w_cut", NHALF, h, 2 * sl + 2)
                need(pe, "proj_read", NG, h, max(st - 1, 0))
                pj = bank[PJ0 + st % 2][:, 0:w]
                for k in range(KT):
                    if first and st < len(GT0):
                        if st + 1 < len(GT0):
                            transpose_first(st + 1, [k])
                        pe.wait_ge(s["hf_ready"], KT * st + k + 1)
                    b = (2 * sl + k // 4) % RING
                    last = parts(pj, w_hi[:, b, k % 4, :], w_lo[:, b, k % 4, :], w_bf[:, b, k % 4, :],
                                 h_hi[:, k, col:col + w], h_lo[:, k, col:col + w], k == 0, k == KT - 1)
                last.then_inc(s["proj_done"], 1)

            def turn_out(h, bi):
                b = (NBLK - 1 - bi) % NBLK
                need(pe, "og_mul", NBLK, h, bi + 1)
                need(pe, "og_ready", NBLK, h, bi)
                for j in range(4):
                    last = pe.transpose(bank[MB][:, j * P:(j + 1) * P], o_t[:, b, j * P:(j + 1) * P], ident[:, :])
                last.then_inc(s["o_tr"], 1)

            def head(h, first, last_head):
                for st in range(NG):
                    project(h, st, first)
                    if 1 <= st <= NV:
                        j = st - 1
                        nt = 2 if j == 0 else 4
                        need(pe, "proj_read", NG, h, st)
                        need(pe, "v_ready", NV, h, j)
                        for i in range(nt):
                            last = pe.transpose(bank[TB][:, i * P:(i + 1) * P], v_t[:, i * P:(i + 1) * P],
                                                ident[:, :])
                        last.then_inc(s["v_tr"], 1)
                    if L0 <= st < L0 + NLATE:
                        i = st - L0
                        if i == 0:
                            need(pe, "head_vec", 2, h, 1)
                            need(pe, "og_ready", NBLK, h, 0)
                        need(pe, "late_in", 16 * NLATE, h, 16 * (i + 1))
                        for j in range(LCOL // P):
                            c = i * (LCOL // P) + j
                            last = pe.matmul(bank[MB][:, c:c + 1], ada1[:, j * P:(j + 1) * P], hv[:, 4:5],
                                             start=(c == 0), stop=True, skip_group_check=True)
                        last.then_inc(s["late_mm"], 1)
                    fi = st - (F0 + 2)
                    if 0 <= fi < NF:
                        need(pe, "x_done", NX, h, fi + 5)
                        if fi == 0:
                            need(pe, "v_ready", NV, h, NV)
                        need(pe, "kt_ready", NF, h, fi)
                        for j in range(2 if lat(fi) is None else 4):
                            last = pe.transpose(bank[TB][:, j * P:(j + 1) * P], kp[:, fi % 2, j * P:(j + 1) * P],
                                                ident[:, :])
                        last.then_inc(s["kt_tr"], 1)
                    fi = st - (F0 + 4)
                    if 0 <= fi < NF and lat(fi) is not None:
                        ai = lat(fi)
                        b = GROUPS[F0 + fi][1]
                        d = 0 if ai < 4 else 1
                        need(pe, "q2_ready", NA, h, ai + 1)
                        need(pe, "w_step", NCHAIN, h, chain_steps(fi) - 1)
                        need(pe, "o_read", NA, h, ai)
                        o = bank[OB]
                        for n in range(8):
                            c = n if d == 0 else 7 - n
                            r = slice(c % 2 * CHUNK, (c % 2 + 1) * CHUNK)
                            pe.matmul(o[r, c // 2 * P:(c // 2 + 1) * P], q2[:, ai % 2, c * CHUNK:(c + 1) * CHUNK],
                                      w_st[:, (8 * ai + n) % 16, :], start=(n < 2), stop=False,
                                      skip_group_check=True)
                        need(pe, "a_masked", NA, h, ai + 1)
                        for j in range(4):
                            last = pe.matmul(o[:, j * P:(j + 1) * P], am[:, 2 * d + ai % 2, j, :],
                                             v_tok[:, 2 + 4 * b + j, :], start=False, stop=True,
                                             skip_group_check=True)
                        last.then_inc(s["o_done"], 1)
                    fi = st - (F0 + 3)
                    if 0 <= fi < NF:
                        ctxb = lat(fi) is None
                        n = 2 if ctxb else 4
                        t0 = 0 if ctxb else 2 + 4 * GROUPS[F0 + fi][1]
                        need(pe, "kt_ready", NF, h, fi + 1)
                        need(pe, "w_step", NCHAIN, h, chain_steps(fi - 1) if fi else 0)
                        for j in range(n):
                            for half in range(2):
                                r = slice(half * CHUNK, (half + 1) * CHUNK)
                                last = pe.matmul(bank[U0 + half][:, j * P:(j + 1) * P], k_tok[r, fi % 2, j, :],
                                                 v_tok[r, t0 + j, :], start=(j == 0), stop=True,
                                                 skip_group_check=True)
                        last.then_inc(s["u_done"], 1)
                    fi = st - (F0 + 2)
                    if 0 <= fi < NF:
                        if lat(fi) is not None:
                            ai = lat(fi)
                            need(pe, "a_masked", NA, h, ai)
                            for j in range(4):
                                last = pe.matmul(bank[AB][:, j * P:(j + 1) * P], kp[:, fi % 2, j * P:(j + 1) * P],
                                                 qp[:, ai % 2, j * P:(j + 1) * P], start=(j == 0), stop=True,
                                                 skip_group_check=True)
                            last.then_inc(s["a_done"], 1)
                    if st == 1 and not first:
                        turn_out(h, -1)
                    if last_head and st == L0 + NLATE:
                        pe.wait_ge(s["late_sum"], HEADS + 1)
                        pe.transpose(bank[MB][0:4 * KT, 0:P], late[:, :], ident[:, :]).then_inc(s["late_tr"], 1)
                    if st == F0 + 11:
                        if last_head:
                            pe.wait_ge(s["late_row"], 1)
                        else:
                            need(pe, "late_sum", 1, h, 2)
                    if st >= F0 + 11:
                        turn_out(h, st - (F0 + 11))

            heads(pe, head)
            turn_out(HEADS, -1)

            def out_proj(layer, i):
                n = NTL * layer + i
                pe.wait_ge(s["olo_ready"], n + 1)
                bf_ready(pe, layer, i)
                if n >= 2:
                    pe.wait_ge(s["yg_ready"], 2 * (n - 1))
                for k in range(KT):
                    if i == 0:
                        pe.wait_ge(s["wo_ready"], KT * layer + k + 1)
                    for j in range(2):
                        c = slice(j * BLK, (j + 1) * BLK)
                        last = parts(bank[(PJ0 if i % 2 == 0 else OB) + j][:, :], og_hi[:, i % 2, k, :],
                                     og_lo[:, i % 2, k, :], og_bf[:, i % 2, k, :], wo_hi[layer][:, k, c],
                                     wo_lo[layer][:, k, c], k == 0, k == KT - 1)
                last.then_inc(s["y_done"], 1)

            for i in range(NTL + 1):
                if i < NTL:
                    out_proj(0, i)
                if i >= 1:
                    n = i - 1
                    pe.wait_ge(s["xn_ready"], n + 1)
                    for j in range(2):
                        if n >= 1:
                            pe.wait_ge(s["hf1_ready"], 2 * n - 1 + j)
                        for k in range(4):
                            last = pe.transpose(bank[TB + j][:, k * P:(k + 1) * P],
                                                xn[:, n % 2, (4 * j + k) * P:(4 * j + k + 1) * P], ident[:, :])
                        last.then_inc(s["tr1_done"], 1)

            pe.wait_ge(s["yg_ready"], 2 * NTL)
            with pe.Fori(0, 2) as pair:
                for par in range(2):
                    g = 2 * pair + par
                    for st in range(4 * NBLK + 1):
                        if st < 4 * NBLK:
                            sl, b = st // NBLK, NBLK - 1 - st % NBLK
                            if st % NBLK == 0:
                                pe.wait_ge(s["pw_cut"], g * 8 + 2 * sl + 2)
                            if par == 0 and st < NBLK:
                                pe.wait_ge(s["h1_ready"], 8 * (st + 1))
                            pe.wait_ge(s["proj_read"], HEADS * NG + g * 16 + max(st - 1, 0))
                            pj = bank[PJ0 + st % 2]
                            for k in range(KT):
                                m = 2 * sl + k // 4
                                last = parts(pj[:, :], pw("hi", m)[:, k % 4, :], pw("lo", m)[:, k % 4, :],
                                             pw("bf", m)[:, k % 4, :], h1_hi[:, k, b * BLK:(b + 1) * BLK],
                                             h1_lo[:, k, b * BLK:(b + 1) * BLK], k == 0, k == KT - 1)
                            last.then_inc(s["proj_done"], 1)
                        if 8 <= st < 12:
                            i = st - 8
                            b = NBLK - 1 - i
                            if i == 0:
                                pe.wait_ge(s[f"wgrp_in{par}"], pair * 16 + 16)
                            pe.wait_ge(s["p_ready"], 1 + g * 8 + NBLK + i + 1)
                            if i:
                                pe.wait_ge(s["y_read"], g * 8 + 2 * i)
                            for o in range(2):
                                for k in range(2):
                                    last = pe.matmul(bank[U0 + o][:, :], wgrp[:, par, k, o * P:(o + 1) * P],
                                                     py[:, par, k, b, :],
                                                     start=(k == 0), stop=(k == 1))
                                last.then_inc(s["y_mm"], 1)

            for i in range(NTL):
                out_proj(1, i)


def kernel(**inputs):
    import numpy as _np
    import concourse.bacc as _bacc
    from concourse import mybir as _mybir
    from concourse.bass_utils import run_bass_kernel_spmd as _run

    a = {k: _np.ascontiguousarray(v) for k, v in inputs.items()}
    rows = [a["ada_b"], a["norm_w"], a["hgrn_gnorm_w"], a["hgrn_lb_logits"], a["pool_scale"], a["c"], a["c_ctx"]]
    key, query = _np.meshgrid(_np.arange(P), _np.arange(P), indexing="ij")
    same = key // CHUNK == query // CHUNK
    mask = _np.stack([same & (key <= query), same & (key >= query)], axis=1).astype(_np.float32)
    t = _np.arange(GRID_W)
    inv = _np.stack([1.0 / (_np.minimum(t - w // 2 + w, GRID_W) - _np.maximum(t - w // 2, 0))
                     for w in WINDOWS]).astype(_np.float32)
    host = [
        ("x", a["x"].reshape(SEQ, D)),
        ("ctx", a["ctx"].reshape(CTX, D)),
        ("ada_w", a["ada_w"]),
        ("ada_late", _np.concatenate([a["ada_w"][0, :, 2 * D:], a["ada_w"][1]], axis=1)
         .reshape(KT, P, NLATE, LCOL).transpose(0, 2, 1, 3)),
        ("vecs", _np.concatenate([r.reshape(-1, P) for r in rows])),
        ("w_in", a["hgrn_w_in"][0].reshape(2, 4, P, NS, HEADS, P)[:, :, :, [W_COL[k] for k in SLICES]]
         .transpose(4, 3, 0, 2, 1, 5).reshape(HEADS, NHALF, P, 4 * P)),
        ("w_out", a["hgrn_w_out"][0]),
        ("pool_w_in", a["pool_w_in"][0]),
        ("pool_w_grp", a["pool_w_grp"][0]),
        ("pool_w_out", a["pool_w_out"][0]),
        ("final_w", a["final_norm_w"].reshape(1, D)),
        ("ident", _np.eye(P, dtype=_np.float32)),
        ("mask", mask),
        ("inv", inv),
    ]
    nc = _bacc.Bacc("TRN2", target_bir_lowering=False, num_devices=1)
    arrays, args = {}, []
    for name, v in host:
        v = _np.ascontiguousarray(v)
        arrays[f"in_{name}"] = v
        args.append(nc.dram_tensor(f"in_{name}", v.shape, _mybir.dt.from_np(v.dtype), kind="ExternalInput").ap())
    args.append(nc.dram_tensor("out_0", (SEQ, D), FP32, kind="ExternalOutput").ap())
    hybrid_kernel(nc, *args)
    r = _run(nc, [arrays], core_ids=[0])
    return r.results[0]["out_0"].reshape(1, SEQ, D)
```
